# Optimizing a Trainium2 kernel written in Bass

```python
import math
import jax, jax.numpy as jnp
from jax import lax
import numpy as np

D_MODEL = 1024
BATCH = 1
SEQ = 512
DEPTH = 1

CHUNK = 64
SSD_HEADS = 8
SSD_HEAD_DIM = 64
SSD_WIDTH = SSD_HEADS * SSD_HEAD_DIM
SSD_GROUPS = 2
SSD_STATE = 128
CONV_WIDTH = 4
XBC_WIDTH = SSD_WIDTH + 2 * SSD_GROUPS * SSD_STATE
HGRN_HEADS = 4
HGRN_HEAD_DIM = 128
HGRN_WIDTH = HGRN_HEADS * HGRN_HEAD_DIM
HGRN_BLOCK = 32
MIX_WIDTH = SSD_WIDTH + HGRN_WIDTH
IN_WIDTH = SSD_WIDTH + XBC_WIDTH + SSD_HEADS + 4 * HGRN_WIDTH
N_EXPERT_GROUPS = 4
EXPERTS_PER_GROUP = 4
N_EXPERTS = N_EXPERT_GROUPS * EXPERTS_PER_GROUP
TOP_K = 2
EXPERT_DIM = 256
EPS = 1e-6

kernel_name = "hymba_ssd_hgrn2_hmoe_trunk"

def rmsnorm(x, w):
    xf = x.astype(jnp.float32)
    y = xf * lax.rsqrt(jnp.mean(xf * xf, axis=-1, keepdims=True) + EPS)
    return (y * w.astype(jnp.float32)).astype(x.dtype)

def causal_depthwise_conv(u, w, b):
    s = u.shape[1]
    up = jnp.pad(u, ((0, 0), (CONV_WIDTH - 1, 0), (0, 0)))
    out = b
    for k in range(CONV_WIDTH):
        out = out + w[k] * up[:, k:k + s]
    return out

def ssd_mixer(z, xbc, dt_raw, conv_w, conv_b, dt_bias, a_log, d_skip, norm_w):
    f32 = jnp.float32
    bsz, s, _ = z.shape
    nc = s // CHUNK
    hpg = SSD_HEADS // SSD_GROUPS
    xbc = jax.nn.silu(causal_depthwise_conv(xbc, conv_w, conv_b))
    xs, bm, cm = jnp.split(xbc, [SSD_WIDTH, SSD_WIDTH + SSD_GROUPS * SSD_STATE], axis=-1)
    xs = xs.astype(f32).reshape(bsz, nc, CHUNK, SSD_GROUPS, hpg, SSD_HEAD_DIM)
    bm = bm.astype(f32).reshape(bsz, nc, CHUNK, SSD_GROUPS, SSD_STATE)
    cm = cm.astype(f32).reshape(bsz, nc, CHUNK, SSD_GROUPS, SSD_STATE)
    dt = jax.nn.softplus(dt_raw.astype(f32) + dt_bias.astype(f32)).reshape(bsz, nc, CHUNK, SSD_GROUPS, hpg)
    a = -jnp.exp(a_log.astype(f32)).reshape(SSD_GROUPS, hpg)
    cum = jnp.cumsum(dt * a, axis=2)
    causal = jnp.tril(jnp.ones((CHUNK, CHUNK), dtype=bool))[None, None, :, :, None, None]
    seg = cum[:, :, :, None] - cum[:, :, None]
    decay = jnp.exp(jnp.where(causal, seg, -jnp.inf))
    cb = jnp.einsum('bctgn,bcsgn->bctsg', cm, bm)
    scores = cb[..., None] * decay * dt[:, :, None]
    y_intra = jnp.einsum('bctsgh,bcsghp->bctghp', scores, xs)
    decay_end = jnp.exp(cum[:, :, -1:] - cum) * dt
    states = jnp.einsum('bcsgn,bcsghp->bcghpn', bm, xs * decay_end[..., None])
    chunk_decay = jnp.exp(cum[:, :, -1])

    def step(h, inp):
        dec, st = inp
        return dec[..., None, None] * h + st, h

    h0 = jnp.zeros((bsz, SSD_GROUPS, hpg, SSD_HEAD_DIM, SSD_STATE), f32)
    _, h_prev = lax.scan(step, h0, (jnp.moveaxis(chunk_decay, 1, 0), jnp.moveaxis(states, 1, 0)))
    h_prev = jnp.moveaxis(h_prev, 0, 1)
    y_inter = jnp.einsum('bctgn,bcghpn->bctghp', cm, h_prev) * jnp.exp(cum)[..., None]
    y = y_intra + y_inter + d_skip.astype(f32).reshape(SSD_GROUPS, hpg)[..., None] * xs
    y = y.reshape(bsz, s, SSD_WIDTH) * jax.nn.silu(z.astype(f32))
    y = y.reshape(bsz, s, SSD_GROUPS, SSD_WIDTH // SSD_GROUPS)
    y = rmsnorm(y, norm_w.reshape(SSD_GROUPS, SSD_WIDTH // SSD_GROUPS))
    return y.reshape(bsz, s, SSD_WIDTH).astype(z.dtype)

def hgrn2_mixer(q, f_logit, i_in, g, lb, norm_w):
    f32 = jnp.float32
    bsz, s, _ = q.shape
    nb = s // HGRN_BLOCK
    shp = (bsz, nb, HGRN_BLOCK, HGRN_HEADS, HGRN_HEAD_DIM)
    forget = lb.astype(f32) + (1.0 - lb.astype(f32)) * jax.nn.sigmoid(f_logit.astype(f32))
    log_f = jnp.log(forget).reshape(shp)
    k = (1.0 - forget).reshape(shp)
    qf = q.astype(f32).reshape(shp)
    v = i_in.astype(f32).reshape(shp)
    b = jnp.cumsum(log_f, axis=2)
    b_ref = b[:, :, HGRN_BLOCK // 2:HGRN_BLOCK // 2 + 1]
    qs = qf * jnp.exp(b - b_ref)
    ks = k * jnp.exp(b_ref - b)
    causal = jnp.tril(jnp.ones((HGRN_BLOCK, HGRN_BLOCK), dtype=bool))
    scores = jnp.where(causal, jnp.einsum('bnthk,bnshk->bnhts', qs, ks), 0.0)
    o_intra = jnp.einsum('bnhts,bnshv->bnthv', scores, v)
    q_dec = qf * jnp.exp(b)
    k_end = k * jnp.exp(b[:, :, -1:] - b)
    blk_decay = jnp.exp(b[:, :, -1])

    def step(state, inp):
        qd, ke, vv, dec = inp
        o = jnp.einsum('bthk,bhkv->bthv', qd, state)
        state = dec[..., None] * state + jnp.einsum('bshk,bshv->bhkv', ke, vv)
        return state, o

    s0 = jnp.zeros((bsz, HGRN_HEADS, HGRN_HEAD_DIM, HGRN_HEAD_DIM), f32)
    _, o_inter = lax.scan(step, s0, (jnp.moveaxis(q_dec, 1, 0), jnp.moveaxis(k_end, 1, 0),
                                     jnp.moveaxis(v, 1, 0), jnp.moveaxis(blk_decay, 1, 0)))
    o = (o_intra + jnp.moveaxis(o_inter, 0, 1)).reshape(bsz, s, HGRN_HEADS, HGRN_HEAD_DIM)
    o = rmsnorm(o, norm_w.reshape(HGRN_HEADS, HGRN_HEAD_DIM)).reshape(bsz, s, HGRN_WIDTH)
    return (o * jax.nn.silu(g.astype(f32))).astype(q.dtype)

def hier_moe(h, router_group, router_expert, w_gate, w_up, w_down):
    f32 = jnp.float32
    bsz, s, d = h.shape
    t = h.reshape(-1, d)
    p_group = jax.nn.softmax((t @ router_group).astype(f32), axis=-1)
    g_idx = jnp.argmax(p_group, axis=-1)
    g_w = jnp.max(p_group, axis=-1)
    logits = (t @ router_expert).astype(f32).reshape(-1, N_EXPERT_GROUPS, EXPERTS_PER_GROUP)
    in_group = jnp.take_along_axis(logits, g_idx[:, None, None], axis=1)[:, 0]
    top_w, top_i = lax.top_k(jax.nn.softmax(in_group, axis=-1), TOP_K)
    top_w = top_w / jnp.sum(top_w, axis=-1, keepdims=True)
    expert_id = g_idx[:, None] * EXPERTS_PER_GROUP + top_i
    combine = jnp.sum(jax.nn.one_hot(expert_id, N_EXPERTS, dtype=f32)
                      * (g_w[:, None] * top_w)[..., None], axis=1)

    def expert_step(acc, inp):
        wg, wu, wd, c = inp
        hid = jax.nn.silu(t @ wg) * (t @ wu)
        return acc + c[:, None].astype(t.dtype) * (hid @ wd), None

    y, _ = lax.scan(expert_step, jnp.zeros_like(t), (w_gate, w_up, w_down, combine.T))
    return y.reshape(bsz, s, d)

def setup_inputs(seed: int = 0) -> dict:
    key = jax.random.key(seed)
    ks = jax.random.split(key, 24)
    f32 = jnp.float32
    nrm = lambda k, shp, sc: jax.random.normal(k, shp, f32) * sc
    dt0 = jnp.exp(jax.random.uniform(ks[5], (DEPTH, SSD_HEADS), f32, math.log(1e-3), math.log(1e-1)))
    return {
        "x": nrm(ks[0], (BATCH, SEQ, D_MODEL), 1.0),
        "norm_mix_w": 1.0 + nrm(ks[1], (DEPTH, D_MODEL), 0.02),
        "w_in": nrm(ks[2], (DEPTH, D_MODEL, IN_WIDTH), D_MODEL ** -0.5),
        "conv_w": nrm(ks[3], (DEPTH, CONV_WIDTH, XBC_WIDTH), CONV_WIDTH ** -0.5),
        "conv_b": nrm(ks[4], (DEPTH, XBC_WIDTH), 0.02),
        "dt_bias": dt0 + jnp.log(-jnp.expm1(-dt0)),
        "a_log": jnp.log(jax.random.uniform(ks[6], (DEPTH, SSD_HEADS), f32, 1.0, 16.0)),
        "d_skip": 1.0 + nrm(ks[7], (DEPTH, SSD_HEADS), 0.1),
        "ssd_norm_w": 1.0 + nrm(ks[8], (DEPTH, SSD_WIDTH), 0.02),
        "hgrn_lb_logits": nrm(ks[9], (DEPTH, HGRN_WIDTH), 0.1),
        "hgrn_norm_w": 1.0 + nrm(ks[10], (DEPTH, HGRN_WIDTH), 0.02),
        "w_out": nrm(ks[11], (DEPTH, MIX_WIDTH, D_MODEL), MIX_WIDTH ** -0.5),
        "norm_ffn_w": 1.0 + nrm(ks[12], (DEPTH, D_MODEL), 0.02),
        "router_group": nrm(ks[13], (DEPTH, D_MODEL, N_EXPERT_GROUPS), D_MODEL ** -0.5),
        "router_expert": nrm(ks[14], (DEPTH, D_MODEL, N_EXPERTS), D_MODEL ** -0.5),
        "w_gate": nrm(ks[15], (DEPTH, N_EXPERTS, D_MODEL, EXPERT_DIM), D_MODEL ** -0.5),
        "w_up": nrm(ks[16], (DEPTH, N_EXPERTS, D_MODEL, EXPERT_DIM), D_MODEL ** -0.5),
        "w_down": nrm(ks[17], (DEPTH, N_EXPERTS, EXPERT_DIM, D_MODEL), EXPERT_DIM ** -0.5),
        "final_norm_w": 1.0 + nrm(ks[18], (D_MODEL,), 0.02),
    }

def reference(x, norm_mix_w, w_in, conv_w, conv_b, dt_bias, a_log, d_skip, ssd_norm_w,
              hgrn_lb_logits, hgrn_norm_w, w_out, norm_ffn_w, router_group, router_expert,
              w_gate, w_up, w_down, final_norm_w):
    p = jax.nn.softmax(hgrn_lb_logits.astype(jnp.float32), axis=0)
    lower_bounds = jnp.cumsum(p, axis=0) - p[0:1]
    splits = [SSD_WIDTH, SSD_WIDTH + XBC_WIDTH, SSD_WIDTH + XBC_WIDTH + SSD_HEADS]
    splits = splits + [splits[-1] + HGRN_WIDTH * j for j in (1, 2, 3)]
    for l in range(DEPTH):
        h = rmsnorm(x, norm_mix_w[l])
        proj = h @ w_in[l]
        z, xbc, dt_raw, hq, hf, hi, hg = jnp.split(proj, splits, axis=-1)
        y_ssd = ssd_mixer(z, xbc, dt_raw, conv_w[l], conv_b[l], dt_bias[l], a_log[l],
                          d_skip[l], ssd_norm_w[l])
        y_hgrn = hgrn2_mixer(hq, hf, hi, hg, lower_bounds[l], hgrn_norm_w[l])
        x = x + jnp.concatenate([y_ssd, y_hgrn], axis=-1) @ w_out[l]
        h = rmsnorm(x, norm_ffn_w[l])
        x = x + hier_moe(h, router_group[l], router_expert[l], w_gate[l], w_up[l], w_down[l])
    return rmsnorm(x, final_norm_w)


_drawn_inputs = setup_inputs


def setup_inputs(seed=0):
    import zlib

    import numpy as np

    out = dict(_drawn_inputs(seed))
    spreads = {}
    factors = {'ssd_norm_w': 3.103, 'hgrn_norm_w': 3.097, 'norm_ffn_w': 2.897, 'final_norm_w': 2.906}
    for name, (base, spread) in spreads.items():
        noise = np.random.default_rng([zlib.crc32(name.encode()), seed]).standard_normal(out[name].shape)
        drawn = base * np.exp(spread * noise) if base else spread * noise
        out[name] = __import__('jax').numpy.asarray(drawn.astype(out[name].dtype))
    for name, factor in factors.items():
        out[name] = (out[name] * factor).astype(out[name].dtype)
    return out
```

```python
from contextlib import ExitStack

import concourse.bass as bass
from concourse import mybir

ALU = mybir.AluOpType
ACT = mybir.ActivationFunctionType
AX_X = mybir.AxisListType.X
F32 = mybir.dt.float32
F32R = mybir.dt.float32r
BF16 = mybir.dt.bfloat16
F16 = mybir.dt.float16
I32 = mybir.dt.int32
U32 = mybir.dt.uint32

P = 128
UNIT = 2048
EPS = 1e-6
BLK = 32
NEG = -1e30
NO_SLOT = 2048
LN_TERMS = (13, 11, 9, 7, 5, 3)


class Chain:

    def __init__(self, eng, sem):
        self.eng, self.sem, self.n = eng, sem, 0

    def mark(self, ins):
        self.n += 1
        ins.then_inc(self.sem, 1)
        return self.n

    def link(self, ins):
        self.mark(ins)
        self.eng.wait_ge(self.sem, self.n)

    def sync(self, n=None):
        self.eng.wait_ge(self.sem, self.n if n is None else n)


def trunk(nc, x, norm_mix_w, w_in, conv_w, conv_b, dt_bias, a_log, d_skip, ssd_norm_w, hgrn_lb_logits,
          hgrn_norm_w, w_out, norm_ffn_w, router_group, router_expert, w_gate, w_up, w_down, final_norm_w, out):
    _, T, D = x.shape
    TT = T // P
    KD = D // P
    CONV = conv_w.shape[1]
    SH = dt_bias.shape[1]
    SW = ssd_norm_w.shape[1]
    XBC = conv_w.shape[2]
    SP = SW // SH
    HW = hgrn_norm_w.shape[1]
    HH = HW // P
    GS = 2
    HPG = SH // GS
    GW = SW // GS
    MT = (SW + HW) // P
    G = router_group.shape[2]
    NE = w_gate.shape[1]
    EG = NE // G
    FE = w_gate.shape[3]
    assert T == 512 and D == 1024 and XBC == SW + 2 * GS * P and HPG * P == 512 and FE == 256

    UC = UNIT // KD
    cz, cx, cdt = 0, SW, SW + XBC
    cq = cdt + SH
    cf, ci, cg = cq + HW, cq + 2 * HW, cq + 3 * HW
    units = [("f", cf), ("f", cf + UC), ("q", cq), ("q", cq + UC), ("i", ci), ("i", ci + UC)]
    units += [("x", cx + j * UC) for j in range(XBC // UC)]
    units += [("g", cg), ("g", cg + UC), ("z", cz), ("z", cz + UC)]
    n_in = len(units)
    units += [("o", j * UC) for j in range(D // UC)]
    n_front = len(units)
    groups = []
    unit_end = []
    for kind, _ in units:
        n = 2 if kind in "fqx" else TT
        groups += [(kind, "act" if kind in "fi" else "dve")] * n
        unit_end.append(len(groups))

    def evacuated(g):
        who = groups[g][1]
        return who, sum(w == who for _, w in groups[:g + 1])

    unit_no = {}
    for n, (kind, _) in enumerate(units):
        unit_no.setdefault(kind, []).append(n)

    U = unit_no
    order = [("unit", U["f"][0]), ("unit", U["f"][1]), ("decay", 0), ("unit", U["q"][0]), ("unit", U["q"][1]),
             ("dt", 0), ("hg_exps", 0), ("unit", U["i"][0]), ("cum", 0), ("unit", U["i"][1]), ("hg_scores", 0),
             ("hg_exps", 1)]
    for j in range(TT):
        order += [("unit", U["x"][j]), ("hg_out", j)]
        if j >= 1:
            order += [("conv_t", 2 * j - 2), ("conv_t", 2 * j - 1)]
        if j + 1 < TT:
            order += [("hg_scores", j + 1)]
        if j + 2 < TT:
            order += [("hg_exps", j + 2)]
    order += [("unit", U["g"][0]), ("ssd_scores", 0), ("unit", U["g"][1]), ("ssd_out", 0), ("ssd_scores", 1),
              ("unit", U["z"][0]), ("ssd_out", 1), ("ssd_scores", 2), ("unit", U["z"][1]), ("ssd_out", 2),
              ("ssd_scores", 3), ("ssd_out", 3)]

    RAW = 3
    SPL = 2

    with ExitStack() as ctx:
        def sb(name, shape, dt=F32):
            return ctx.enter_context(nc.sbuf_tensor(name, shape, dt))

        def sem(name):
            return ctx.enter_context(nc.semaphore(name))

        raw = sb("raw", [P, RAW, UNIT])
        wh = sb("wh", [P, SPL, UNIT], F32R)
        wl = sb("wl", [P, SPL, UNIT], F32R)
        acth = sb("acth", [P, KD * T], F32R)
        actl = sb("actl", [P, KD * T], F32R)
        bc = sb("bc", [P, D])
        X = sb("X", [P, TT, D])
        arena = sb("arena", [P, 23552])
        ident = sb("ident", [P, P])
        identb = sb("identb", [P, P], BF16)
        ones = sb("ones", [P, P])
        upto = sb("upto", [P, P])
        negm = sb("negm", [P, P], BF16)
        blockm = sb("blockm", [P, P])
        rows = sb("rows", [P, P])
        cols = sb("cols", [P, 52])
        hc = sb("hc", [P, 40])
        lb = sb("lb", [P, 4, HH])
        bc8 = sb("bc8", [P, 3, SH])
        dtw = sb("dtw", [P, KD * SH])
        dtwh = sb("dtwh", [P, KD * SH], F32R)
        dtwl = sb("dtwl", [P, KD * SH], F32R)
        sm = sb("sm", [P, 16, TT * SH])
        st = sb("st", [P, 6, 24])
        dec = sb("dec", [P, 2, HH])
        hidh = sb("hidh", [P, FE], F32R)
        hidl = sb("hidl", [P, FE], F32R)
        rt = sb("rt", [P, KD, G + NE])
        reset = sb("reset", [P, 2, T], BF16)

        ofs = [0]

        def part(n):
            a = ofs[0]
            ofs[0] += n
            return arena[:, a:a + n]

        W = HH * P
        q = part(TT * W).rearrange("p (t n) -> p t n", t=TT)
        kk = part(TT * W).rearrange("p (t n) -> p t n", t=TT)
        lf = part(TT * W).rearrange("p (t n) -> p t n", t=TT)
        v = part(TT * HW).rearrange("p (t n) -> p t n", t=TT)
        xs = part(TT * SW).rearrange("p (t n) -> p t n", t=TT)
        bct = part(4 * T).rearrange("p (j n) -> p j n", j=4)
        btok = part(TT * GS * P).rearrange("p (t n) -> p t n", t=TT)
        conv0 = ofs[0]
        cvx = part(2 * T).rearrange("p (b n) -> p b n", b=2)
        acc = part(2 * T).rearrange("p (b n) -> p b n", b=2)
        th = part(T)
        b32, b128, ep, en, x32, x64, ke = (part(W) for _ in range(7))
        qb = part(2 * W).rearrange("p (b n) -> p b n", b=2)
        sct = part(2 * W).rearrange("p (b n) -> p b n", b=2)
        ket = part(W)
        S = part(W)
        sq = part(W)
        hs = part(SW)
        assert ofs[0] <= 23552
        E = arena[:, conv0:conv0 + SH * P]
        xdt = arena[:, conv0 + 1024:conv0 + 1536]
        xw = arena[:, conv0 + 1536:conv0 + 2048]
        yt = arena[:, conv0 + 2048:conv0 + 2560]
        sg, sz = q, lf
        xres = arena[:, 0:TT * D].rearrange("p (t n) -> p t n", t=TT)

        ofs[0] = TT * D
        raw_a = [raw[:, 0, :], raw[:, 1, :]]
        raw_b = [raw[:, 2, :], part(UNIT)]
        raw_c = [part(UNIT), part(UNIT)]
        hg = part(2 * D).rearrange("p (b n) -> p b n", b=2)
        ysb = part(2 * D).rearrange("p (b n) -> p b n", b=2)
        h2t = part(2 * D).rearrange("p (b n) -> p b n", b=2)
        onehot = part(TT * P // 2).bitcast(F16).rearrange("p (t s) -> p t s", t=TT)
        vals = part(TT * NE).bitcast(F16).rearrange("p (t e c) -> p t e c", t=TT, c=2)
        vale = part(TT).bitcast(F16).rearrange("p (t c) -> p t c", t=TT)
        sil = part(FE)
        hid = part(FE)
        iota1 = part(P)
        iotai = part(P).bitcast(I32)
        tokc = part(TT)
        prio = part(EG)
        lg = part(TT * (G + NE)).rearrange("p (t n) -> p t n", t=TT)
        r4 = part(12 * TT * 4).rearrange("p (i t n) -> p i t n", i=12, t=TT)
        r1 = part(12 * TT).rearrange("p (i t) -> p i t", i=12)
        r16 = part(5 * TT * NE).rearrange("p (i t n) -> p i t n", i=5, t=TT)
        mb = part(TT * NE // 2).bitcast(BF16).rearrange("p (t n) -> p t n", t=TT)
        before = part(P // 2).bitcast(BF16)
        onesb = part(P // 2).bitcast(BF16)
        gix = part(2).bitcast(I32)
        six = part(NE).bitcast(I32)
        sixe = part(2).bitcast(I32)
        rnd = part(4)
        rounds = part(1).bitcast(I32)
        pairs = arena[:, TT * D:TT * D + 2 * TT * D].rearrange("p (t c n) -> p t c n", t=TT, c=2)
        assert ofs[0] <= 23552
        wch, wcl = acth[:, 0:UNIT], actl[:, 0:UNIT]
        gth = [acth[:, UNIT + b * D:UNIT + (b + 1) * D] for b in range(2)]
        gtl = [actl[:, UNIT + b * D:UNIT + (b + 1) * D] for b in range(2)]

        bank = [ctx.enter_context(nc.psum_tensor(f"bank{i}", [P, 512], F32)) for i in range(8)]

        x_in = [sem(f"x_in{i}") for i in range(TT)]
        bc_in = sem("bc_in")
        const_in = sem("const_in")
        raw_in = [sem(f"raw_in{i}") for i in range(RAW)]
        xres_in = sem("xres_in")
        out_st = sem("out_st")

        pool_step = sem("pool_step")
        dve_step = sem("dve_step")
        act_step = sem("act_step")
        const_ok = sem("const_ok")
        ssq_ok = sem("ssq_ok")
        std_ok = sem("std_ok")
        rms_ok = sem("rms_ok")
        h_ok = sem("h_ok")
        tr_ok = sem("tr_ok")
        ah_ok = sem("ah_ok")
        al_ok = sem("al_ok")
        cols_t = sem("cols_t")
        hc_ok = sem("hc_ok")
        wh_ok = sem("wh_ok")
        wl_ok = sem("wl_ok")
        grp = sem("grp")
        ev_act = sem("ev_act")
        ev_dve = sem("ev_dve")
        sgm_ok = sem("sgm_ok")
        dtw_h = sem("dtw_h")
        dtw_l = sem("dtw_l")
        dt_mm = sem("dt_mm")
        dt_abs = sem("dt_abs")
        dt_exp = sem("dt_exp")
        dA_ok = sem("dA_ok")
        cum_mm = sem("cum_mm")
        cum_ok = sem("cum_ok")
        cum_exp = sem("cum_exp")
        dts_ok = sem("dts_ok")
        hg_sub = sem("hg_sub")
        hg_exp = sem("hg_exp")
        hg_ops = sem("hg_ops")
        hg_sc = sem("hg_sc")
        hg_sa = sem("hg_sa")
        hg_sb = sem("hg_sb")
        hg_o = sem("hg_o")
        hg_kv = sem("hg_kv")
        hg_sq = sem("hg_sq")
        hg_ev = sem("hg_ev")
        hg_st = sem("hg_st")
        cv_acc = sem("cv_acc")
        cv_th = sem("cv_th")
        cv_ok = sem("cv_ok")
        cv_t = sem("cv_t")
        cv_ev = sem("cv_ev")
        gt_th = sem("gt_th")
        ss_mm = sem("ss_mm")
        ss_seg = sem("ss_seg")
        ss_exp = sem("ss_exp")
        ss_m = sem("ss_m")
        ss_y = sem("ss_y")
        ss_h = sem("ss_h")
        ss_ev = sem("ss_ev")
        hs_ok = sem("hs_ok")
        yz_ok = sem("yz_ok")
        yg_ok = sem("yg_ok")
        bc2_in = sem("bc2_in")
        bc3_in = sem("bc3_in")
        h2_st = sem("h2_st")
        rt_in = sem("rt_in")
        moe_mem = sem("moe_mem")
        h2_ok = sem("h2_ok")
        h2_tr = sem("h2_tr")
        h2_ev = sem("h2_ev")
        lg_mm = sem("lg_mm")
        ge_in = sem("ge_in")
        ge_ok = sem("ge_ok")
        e2_in = sem("e2_in")
        e2_ok = sem("e2_ok")
        m_ok = sem("m_ok")
        pos_mm = sem("pos_mm")
        routed = sem("routed")
        y_free = sem("y_free")
        q_ok = sem("q_ok")
        ix_mm = sem("ix_mm")
        ix_ok = sem("ix_ok")
        g_tr = sem("g_tr")
        gh_ok = sem("gh_ok")
        gl_ok = sem("gl_ok")
        wha_ok = sem("wha_ok")
        whb_ok = sem("whb_ok")
        whc_ok = sem("whc_ok")
        wla_ok = sem("wla_ok")
        wlb_ok = sem("wlb_ok")
        wlc_ok = sem("wlc_ok")
        gu_a = sem("gu_a")
        gu_b = sem("gu_b")
        sil_ok = sem("sil_ok")
        hid_ok = sem("hid_ok")
        hid_tr = sem("hid_tr")
        hh_ok = sem("hh_ok")
        hl_ok = sem("hl_ok")
        dn = sem("dn")
        y0_ok = sem("y0_ok")
        y1_ok = sem("y1_ok")
        next_ok = sem("next_ok")
        six_ok = sem("six_ok")
        pool_tick = sem("pool_tick")
        res_ok = sem("res_ok")
        fsq_ok = sem("fsq_ok")
        fms_ok = sem("fms_ok")
        fsd_ok = sem("fsd_ok")
        fin_ok = sem("fin_ok")
        ra_in, rb_in, rc_in, gat_in, sca_out = ([sem(f"{n}{b}") for b in range(2)]
                                                for n in ("ra_in", "rb_in", "rc_in", "gat_in", "sca_out"))
        pair_in = [sem(f"pair_in{t}") for t in range(TT)]

        h2_dram = nc.dram_tensor("h2_dram", (T, D), F32, kind="Internal").ap()
        pairs_dram = nc.dram_tensor("pairs_dram", (2 * T, D), F32, kind="Internal").ap()
        AHEAD_DVE = ((gl_ok, 2), (hl_ok, 1), (hid_ok, 1), (y1_ok, 1))
        PAIRS = NE // 2
        CAP = P

        def expert_rounds(eng, body):
            eng.wait_ge(routed, 1)
            n = eng.value_load(rounds[0:1, 0:1], min_val=1, max_val=T // CAP)
            with eng.Fori(0, n) as r:
                body(r, r * NE)
            return n

        def front_src(u):
            kind, c = units[u]
            w = w_out if kind == "o" else w_in
            return w[0, :, c:c + UC].rearrange("(k p) n -> p k n", p=P)

        def raw3(slot):
            return raw[:, slot, :].rearrange("p (k n) -> p k n", k=KD)

        block = ctx.enter_context(nc.Block())

        @block.sync
        def _(sp):
            for tt in range(TT):
                sp.dma_start(X[:, tt, :], x[0, tt * P:(tt + 1) * P, :]).then_inc(x_in[tt], 16)
                if tt == 0:
                    sp.dma_start(bc[:, :], norm_mix_w[0:1, :].broadcast_to([P, D])).then_inc(bc_in, 16)
            sp.dma_start(raw3(0), front_src(0)).then_inc(raw_in[0], 16)
            n = 0
            for dst, src in (
                (rows[0:32, :], conv_w[0].rearrange("k (f p) -> (k f) p", p=P)),
                (rows[32:40, :], conv_b[0].rearrange("(f p) -> f p", p=P)),
                (rows[40:44, :], ssd_norm_w[0].rearrange("(f p) -> f p", p=P)),
                (rows[44:48, :], hgrn_norm_w[0].rearrange("(f p) -> f p", p=P)),
                (rows[48:52, :], hgrn_lb_logits[0].rearrange("(f p) -> f p", p=P)),
                (bc8[:, 0, :], dt_bias[0:1, :].broadcast_to([P, SH])),
                (bc8[:, 1, :], a_log[0:1, :].broadcast_to([P, SH])),
                (bc8[:, 2, :], d_skip[0:1, :].broadcast_to([P, SH])),
                (dtw[:, :].rearrange("p (k n) -> p k n", k=KD),
                 w_in[0, :, cdt:cdt + SH].rearrange("(k p) n -> p k n", p=P)),
            ):
                sp.dma_start(dst, src).then_inc(const_in, 16)
                n += 1
            assert n == 9
            for u in range(1, n_front):
                if u >= RAW:
                    sp.wait_ge(wl_ok, u - RAW + 1)
                sp.dma_start(raw3(u % RAW), front_src(u)).then_inc(raw_in[u % RAW], 16)
            sp.wait_ge(yg_ok, TT)
            sp.dma_start(xres, x[0].rearrange("(t p) n -> p t n", p=P)).then_inc(xres_in, 16)
            sp.wait_ge(h_ok, TT)
            sp.dma_start(bc[:, :], norm_ffn_w[0:1, :].broadcast_to([P, D])).then_inc(bc2_in, 16)
            sp.dma_start(rt[:, :, 0:G], router_group[0].rearrange("(k p) n -> p k n", p=P)).then_inc(rt_in, 16)
            sp.dma_start(rt[:, :, G:G + NE], router_expert[0].rearrange("(k p) n -> p k n", p=P)).then_inc(rt_in, 16)

            def load_expert(e, b, step):
                kh = KD // 2
                for h, (dst, into, split) in enumerate(((raw_a[b], ra_in[b], wla_ok), (raw_b[b], rb_in[b], wlb_ok))):
                    if step is not None:
                        sp.wait_ge(split, (step - 1) * 2)
                    d3 = dst.rearrange("p (k n) -> p k n", k=kh)
                    for n, w in enumerate((w_gate, w_up)):
                        src = w[0, bass.ds(e, 1), h * kh * P:(h + 1) * kh * P, :]
                        sp.dma_start(d3[:, :, n * FE:(n + 1) * FE],
                                     src.rearrange("o (k p) f -> p (o k) f", p=P)).then_inc(into, 16)
                if step is not None:
                    sp.wait_ge(wlc_ok, (step - 1) * 2)
                sp.dma_start(raw_c[b].rearrange("p (k n) -> p k n", k=FE // P),
                             w_down[0, bass.ds(e, 1), :, :].rearrange("o (k p) d -> p (o k) d", p=P)).then_inc(rc_in[b], 16)

            sp.wait_ge(wl_ok, n_front)
            load_expert(0, 0, None)
            load_expert(1, 1, None)
            with sp.Fori(1, PAIRS) as pp:
                for b in range(2):
                    load_expert(pp * 2 + b, b, pp * 2 + b)
            sp.wait_ge(h2_ok, TT)
            sp.dma_start(bc[:, :], final_norm_w[None, :].broadcast_to([P, D])).then_inc(bc3_in, 16)
            sp.wait_ge(routed, 1)
            n = sp.value_load(rounds[0:1, 0:1], min_val=1, max_val=T // CAP)
            with sp.If(n > 1):
                with sp.Fori(1, n) as r:
                    with sp.Fori(0, PAIRS) as pp:
                        for b in range(2):
                            load_expert(pp * 2 + b, b, r * NE + pp * 2 + b)
            for b in range(2):
                sp.wait_ge(sca_out[b], n * (16 * PAIRS))
            for tt in range(TT):
                sp.dma_start(pairs[:, tt, :, :], pairs_dram.rearrange("(c t p) n -> t p c n", c=2, p=P)[tt])\
                    .then_inc(pair_in[tt], 16)
            for tt in range(TT):
                sp.wait_ge(fin_ok, tt + 1)
                sp.dma_start(out[0, tt * P:(tt + 1) * P, :], xres[:, tt, :]).then_inc(out_st, 16)
            sp.wait_ge(out_st, 16 * TT)

        @block.gpsimd
        def _(pool):
            ch = Chain(pool, pool_step)
            gp = nc.gpsimd
            gp.memset(ident[:, :], 0.0)
            gp.memset(identb[:, :], 0.0)
            gp.memset(ones[:, :], 1.0)
            gp.memset(upto[:, :], 1.0)
            gp.memset(negm[:, :], 0.0)
            gp.memset(reset[:, :, :], 1.0)
            ch.link(gp.memset(blockm[:, :], 1.0))
            for m in (ident, identb):
                gp.affine_select(out=m[:, :], in_=m[:, :], compare_op=ALU.not_equal, fill=1.0, base=0,
                                 pattern=[[-1, P]], channel_multiplier=1)
            gp.affine_select(out=upto[:, :], in_=upto[:, :], compare_op=ALU.is_ge, fill=0.0, base=0,
                             pattern=[[1, P]], channel_multiplier=-1)
            gp.affine_select(out=negm[:, :], in_=negm[:, :], compare_op=ALU.is_ge, fill=NEG, base=0,
                             pattern=[[1, P]], channel_multiplier=-1)
            ch.link(gp.affine_select(out=blockm[:, :], in_=blockm[:, :], compare_op=ALU.is_ge, fill=0.0, base=0,
                                     pattern=[[1, P]], channel_multiplier=-1))
            bm = blockm[:, :].rearrange("p (n c) -> p n c", c=BLK)
            gp.affine_select(out=bm, in_=bm, compare_op=ALU.is_ge, fill=0.0, base=0,
                             pattern=[[-BLK, P // BLK], [0, BLK]], channel_multiplier=1)
            gp.memset(reset[:, 0, :].rearrange("p (n c) -> p n c", c=BLK)[:, :, 0:1], 0.0)
            gp.memset(sct[:, :, :], 0.0)
            gp.memset(reset[:, 1, :].rearrange("p (n c) -> p n c", c=P)[:, :, 0:1], 0.0).then_inc(const_ok, 1)

            pool.wait_ge(dtw_h, 1)
            gp.tensor_tensor(dtwl[:, :], dtw[:, :], dtwh[:, :].bitcast(F32), ALU.subtract).then_inc(dtw_l, 1)
            for u in range(n_front):
                pool.wait_ge(wh_ok, u + 1)
                gp.tensor_tensor(wl[:, u % SPL, :], raw[:, u % RAW, :], wh[:, u % SPL, :].bitcast(F32),
                                 ALU.subtract).then_inc(wl_ok, 1)
            pool.wait_ge(yg_ok, TT)
            gp.memset(hg[:, :, :], 0.0)
            gp.memset(onesb, 1.0)
            gp.memset(before, 1.0)
            for i in range(EG):
                gp.memset(prio[:, i:i + 1], float(EG - i))
            ch.link(gp.iota(iotai, [[1, P]], base=1, channel_multiplier=0))
            ch.link(gp.tensor_copy(iota1, iotai))
            ch.link(gp.iota(iotai[:, 0:TT], [[P, TT]], base=-NO_SLOT, channel_multiplier=1))
            gp.tensor_copy(tokc, iotai[:, 0:TT])
            gp.affine_select(out=before, in_=before, compare_op=ALU.is_ge, fill=0.0, base=-1, pattern=[[1, P]],
                             channel_multiplier=-1).then_inc(moe_mem, 1)

            def gather(step, b, first=False):
                pool.wait_ge(ix_ok, step + 1)
                pool.sem_inc(pool_tick, 1)
                gp.indirect_dma_start(hg[:, b, :], None, h2_dram, bass.IndirectOffsetOnAxis(ap=gix[:, b:b + 1], axis=0),
                                      bounds_check=T - 1, oob_is_err=False).then_inc(gat_in[b], 16)

            def split_a(step, b):
                for h in range(2):
                    c = slice(h * UNIT // 2, (h + 1) * UNIT // 2)
                    pool.wait_ge(wha_ok, step * 2 + (h + 1))
                    gp.tensor_tensor(wl[:, 0, c], raw_a[b][:, c], wh[:, 0, c].bitcast(F32),
                                     ALU.subtract).then_inc(wla_ok, 1)

            def scatter(e, step, b):
                pool.wait_ge(y0_ok, step + 2)
                pool.wait_ge(y1_ok, step + 2)
                pool.sem_inc(pool_tick, 1)
                gp.tensor_copy(sixe[:, b:b + 1], six[:, bass.ds(e, 1)]).then_inc(six_ok, 1)
                pool.wait_ge(six_ok, step + 1)
                pool.sem_inc(pool_tick, 1)
                gp.indirect_dma_start(pairs_dram, bass.IndirectOffsetOnAxis(ap=sixe[:, b:b + 1], axis=0),
                                      ysb[:, b, :], None, bounds_check=2 * T - 1, oob_is_err=False)\
                    .then_inc(sca_out[b], 16)

            def expert_step(e, step, b, uses, ahead2, ahead3):
                if ahead2:
                    split_a(step + 2, b)
                if ahead3:
                    gather(step + 3, 1 - b)
                scatter(e, step, b)
                pool.wait_ge(sca_out[b], uses * 16)
                pool.sem_inc(y_free, 1)

            def pool_round(r, base):
                gather(base, 0)
                gather(base + 1, 1)
                split_a(base, 0)
                split_a(base + 1, 1)
                gather(base + 2, 0)
                used = r * PAIRS
                with pool.Fori(0, PAIRS - 2) as pp:
                    for b in range(2):
                        expert_step(pp * 2 + b, base + pp * 2 + b, b, used + pp + 1, True, True)
                for e in range(NE - 4, NE):
                    expert_step(e, base + e, e % 2, used + e // 2 + 1, e + 2 < NE, e + 3 < NE)

            pool.wait_ge(h2_st, 16 * TT)
            pool.sem_inc(y_free, 2)
            expert_rounds(pool, pool_round)

        def h4(ap):
            return ap.rearrange("p (m s c) -> p m s c", s=2, c=BLK)

        @block.scalar
        def _(act):
            sc = nc.scalar
            ch = Chain(act, act_step)
            n_tr = [0]

            def round_unit(u):
                act.wait_ge(raw_in[u % RAW], 16 * (u // RAW + 1))
                if u >= SPL:
                    act.wait_ge(grp, unit_end[u - SPL])
                sc.activation(wh[:, u % SPL, :], raw[:, u % RAW, :], ACT.Copy).then_inc(wh_ok, 1)

            for tt in range(TT):
                act.wait_ge(x_in[tt], 16)
                sc.activation(arena[:, tt * D:(tt + 1) * D], X[:, tt, :], ACT.Square,
                               accum_out=st[:, 0, tt:tt + 1]).then_inc(ssq_ok, 1)
            act.wait_ge(rms_ok, 1)
            sc.activation(st[:, 2, 0:TT], st[:, 1, 0:TT], ACT.Sqrt).then_inc(std_ok, 1)
            act.wait_ge(const_in, 16 * 9)
            sc.activation(dtwh[:, :], dtw[:, :], ACT.Copy).then_inc(dtw_h, 1)
            round_unit(0)
            for i in range(2 * TT):
                act.wait_ge(tr_ok, i + 1)
                tt, half = i // 2, i % 2
                dst = acth[:, :].rearrange("p (k t) -> p k t", k=KD)[:, 4 * half:4 * half + 4, tt * P:(tt + 1) * P]
                sc.activation(dst, bank[i][:, :].rearrange("p (k t) -> p k t", k=4), ACT.Copy).then_inc(ah_ok, 1)
            round_unit(1)
            act.wait_ge(hc_ok, 1)
            lbc = cols[:, 48:52]
            ch.link(sc.activation(lb[:, 3, :], lb[:, 0, :], ACT.Exp))
            g = 0
            for what, n in order:
                if what == "unit":
                    kind, c = units[n]
                    for j in range(2 if kind in "fqx" else TT):
                        if kind == "f":
                            act.wait_ge(grp, g + 1)
                            hd = (n - U["f"][0]) * 2 + j
                            sc.activation(kk[:, :, hd * P:(hd + 1) * P],
                                          bank[g % 2][:, :].rearrange("p (t n) -> p t n", t=TT),
                                          ACT.Sigmoid).then_inc(ev_act, 1)
                        elif kind == "i":
                            act.wait_ge(grp, g + 1)
                            c0 = (n - U["i"][0]) * UC
                            sc.activation(v[:, j, c0:c0 + UC], bank[g % 2][:, 0:UC], ACT.Copy).then_inc(ev_act, 1)
                        elif kind == "x":
                            jj = (n - U["x"][0]) * 2 + j
                            act.wait_ge(cv_acc, jj + 1)
                            sc.activation(th, acc[:, jj % 2, :], ACT.Tanh).then_inc(cv_th, 1)
                        elif kind in "gz":
                            k = (n - U["g"][0]) * TT + j
                            act.wait_ge(grp, g + 1)
                            if k == 0:
                                act.wait_ge(hg_ev, TT)
                            else:
                                act.wait_ge(ev_dve, evacuated(g - 1)[1])
                            sc.activation(sq[:, 0:UC], bank[g % 2][:, 0:UC], ACT.Tanh,
                                          scale=0.5).then_inc(gt_th, 1)
                        g += 1
                    if n + SPL < n_front:
                        round_unit(n + SPL)
                elif what == "decay":
                    act.wait_ge(hc_ok, 2)
                    act.wait_ge(ev_act, 4)
                    for hd in range(HH):
                        last = sc.activation(lf[:, :, hd * P:(hd + 1) * P], kk[:, :, hd * P:(hd + 1) * P], ACT.Ln,
                                             scale=lb[:, 1, hd:hd + 1], bias=lb[:, 0, hd:hd + 1])
                    last.then_inc(sgm_ok, 1)
                elif what == "dt":
                    act.wait_ge(dt_abs, 1)
                    sc.activation(sm[:, 9, 0:SH], bc8[:, 1, :], ACT.Exp)
                    sc.activation(sm[:, 2, :], sm[:, 1, :], ACT.Exp, scale=-1.0).then_inc(dt_exp, 1)
                elif what == "cum":
                    act.wait_ge(cum_ok, 1)
                    sc.activation(sm[:, 12, :], sm[:, 10, :], ACT.Exp)
                    sc.activation(sm[:, 13, :], sm[:, 11, :], ACT.Exp)
                    sc.activation(sm[:, 14, :], sm[:, 14, :], ACT.Exp).then_inc(cum_exp, 1)
                elif what == "hg_exps":
                    i = n
                    act.wait_ge(hg_sub, i + 1)
                    sc.activation(en, ep, ACT.Exp, scale=-1.0)
                    if i >= 2:
                        act.wait_ge(hg_kv, i - 1)
                    sc.activation(qb[:, i % 2, :], b128, ACT.Exp)
                    sc.activation(h4(x32)[:, :, 1, :], h4(b32)[:, :, 1, :], ACT.Exp)
                    sc.activation(h4(x32)[:, :, 0, :], h4(x32)[:, :, 0, :], ACT.Exp)
                    m2 = x64.rearrange("p (h s c) -> p h s c", s=2, c=2 * BLK)
                    sc.activation(m2[:, :, 0, :], m2[:, :, 0, :], ACT.Exp, scale=-1.0)
                    sc.activation(m2[:, :, 1, :], m2[:, :, 1, :], ACT.Exp)
                    if i >= 2:
                        act.wait_ge(hg_st, i - 1)
                    sc.activation(dec[:, i % 2, :], b128.rearrange("p (h t) -> p h t", h=HH)[:, :, P - 1], ACT.Exp)
                    ch.link(sc.activation(ke, ke, ACT.Exp))
                    sc.activation(ep, ep, ACT.Exp).then_inc(hg_exp, 1)
                elif what == "hg_scores":
                    i = n
                    act.wait_ge(hg_sc, i + 1)
                    act.wait_ge(hg_sa, i + 1)
                    dst = sct[:, i % 2, :].rearrange("p (h t) -> p h t", h=HH)
                    src = bank[4][:, :].rearrange("p (h t) -> p h t", h=HH)
                    sc.activation(dst[0:64, :, 64:128], src[0:64, :, 64:128], ACT.Copy)
                    sc.activation(dst[0:32, :, 32:64], src[0:32, :, 32:64], ACT.Copy)
                    sc.activation(dst[64:96, :, 96:128], src[64:96, :, 96:128], ACT.Copy)
                    sc.activation(ket, bank[2][:, :], ACT.Copy).then_inc(hg_sb, 1)
                elif what == "hg_out":
                    i = n
                    act.wait_ge(hg_o, i + 1)
                    if i >= 1:
                        act.wait_ge(hg_ev, i)
                    sc.activation(sq, bank[5][:, :], ACT.Square).then_inc(hg_sq, 1)
                elif what == "conv_t":
                    j = n
                    act.wait_ge(cv_t, j + 1)
                    src = bank[7 if j % 2 else 2][:, :].rearrange("p (t n) -> p t n", t=TT)
                    dst = xs[:, :, j * P:(j + 1) * P] if j < 4 else btok[:, :, (j - 4) * P:(j - 3) * P]
                    sc.activation(dst, src, ACT.Copy).then_inc(cv_ev, 1)
                elif what == "ssd_scores":
                    act.wait_ge(ss_seg, n + 1)
                    sc.activation(E, E, ACT.Exp).then_inc(ss_exp, 1)
            for tt in range(TT):
                act.wait_ge(yz_ok, tt + 1)
                for gr in range(GS):
                    last = sc.activation(sq[:, 0:GW], X[:, tt, gr * GW:(gr + 1) * GW], ACT.Square,
                                         accum_out=st[:, 3, 16 + tt * GS + gr:17 + tt * GS + gr])
                    if (tt, gr) == (TT - 1, GS - 1):
                        last.then_inc(ssq_ok, 1)
                    else:
                        ch.link(last)
            act.wait_ge(rms_ok, 2)
            sc.activation(st[:, 5, :], st[:, 4, :], ACT.Sqrt).then_inc(std_ok, 1)
            for f in range(MT):
                act.wait_ge(tr_ok, 2 * TT + f + 1)
                sc.activation(acth[:, f * T:(f + 1) * T], bank[f][:, :], ACT.Copy,
                              scale=cols[:, 40 + f:41 + f]).then_inc(ah_ok, 1)
            for u in range(n_in, n_front):
                if u + SPL < n_front:
                    round_unit(u + SPL)
            act.wait_ge(ev_dve, evacuated(len(groups) - 1)[1])
            for tt in range(TT):
                sc.activation(X[:, tt, :], xres[:, tt, :], ACT.Square, accum_out=st[:, 0, tt:tt + 1]).then_inc(ssq_ok, 1)
            act.wait_ge(rms_ok, 3)
            sc.activation(st[:, 5, 0:TT], st[:, 4, 0:TT], ACT.Sqrt).then_inc(std_ok, 1)

            def halves(b2):
                return [(slice(h * UNIT // 2, (h + 1) * UNIT // 2)) for h in b2]

            def round_a(step, b, uses):
                act.wait_ge(ra_in[b], uses * 32)
                for c in halves((0, 1)):
                    sc.activation(wh[:, 0, c], raw_a[b][:, c], ACT.Copy).then_inc(wha_ok, 1)

            def round_b(step, b, uses, hs_=(0, 1)):
                act.wait_ge(rb_in[b], uses * 32)
                for c in halves(hs_):
                    sc.activation(wh[:, 1, c], raw_b[b][:, c], ACT.Copy).then_inc(whb_ok, 1)

            def round_c(step, b, uses):
                act.wait_ge(dn, step * 2 + 2)
                act.wait_ge(rc_in[b], uses * 16)
                for c in halves((0, 1)):
                    sc.activation(wch[:, c], raw_c[b][:, c], ACT.Copy).then_inc(whc_ok, 1)

            for tt in range(TT):
                act.wait_ge(h2_ok, tt + 1)
                act.dma_start(h2_dram[tt * P:(tt + 1) * P, :], X[:, tt, :]).then_inc(h2_st, 16)
            act.wait_ge(ge_in, 1)
            sc.activation(r4[:, 1], r4[:, 0], ACT.Exp).then_inc(ge_ok, 1)
            act.wait_ge(e2_in, 1)
            sc.activation(r1[:, 4], r1[:, 3], ACT.Exp).then_inc(e2_ok, 1)
            ch.link(sc.activation(dec[:, 0, 0:1], ident[:, 0:1], ACT.Silu))

            def round_tokens(step, b):
                for h in range(2):
                    act.wait_ge(g_tr, step * 2 + (h + 1))
                    sc.activation(gth[b][:, h * 512:(h + 1) * 512], bank[2 + h][:, :], ACT.Copy).then_inc(gh_ok, 1)

            def act_step_(e, step, b, uses, ahead1, ahead2):
                o = 1 - b
                uses1 = uses + b
                if ahead1:
                    round_tokens(step + 1, o)
                round_c(step, b, uses)
                act.wait_ge(gu_b, step + 1)
                sc.activation(sil, bank[b][:, 0:FE], ACT.Silu).then_inc(sil_ok, 1)
                if ahead1:
                    round_b(step + 1, o, uses1, (0,))
                act.wait_ge(hid_tr, step + 1)
                sc.activation(hidh[:, :], bank[4][:, 0:FE], ACT.Copy).then_inc(hh_ok, 1)
                if ahead1:
                    round_b(step + 1, o, uses1, (1,))
                if ahead2:
                    act.wait_ge(gu_a, step + 2)
                    round_a(step + 2, b, uses + 1)
                act.wait_ge(dn, step * 2 + 3)
                act.wait_ge(y_free, step + 1)
                sc.activation(ysb[:, b, 0:512], bank[5][:, :], ACT.Copy).then_inc(y0_ok, 1)

            def act_round(r, base):
                used = r * PAIRS
                round_a(base, 0, used + 1)
                round_b(base, 0, used + 1)
                round_tokens(base, 0)
                act.wait_ge(gu_a, base + 1)
                round_a(base + 1, 1, used + 1)
                with act.Fori(0, PAIRS - 1) as pp:
                    for b in range(2):
                        act_step_(pp * 2 + b, base + pp * 2 + b, b, used + pp + 1, True, True)
                act_step_(NE - 2, base + NE - 2, 0, used + PAIRS, True, False)
                act_step_(NE - 1, base + NE - 1, 1, used + PAIRS, False, False)

            act.sem_inc(y0_ok, 1)
            expert_rounds(act, act_round)
            for tt in range(TT):
                act.wait_ge(res_ok, tt + 1)
                sc.activation(X[:, tt, :], xres[:, tt, :], ACT.Square, accum_out=st[:, 0, tt:tt + 1]).then_inc(fsq_ok, 1)
                act.wait_ge(fms_ok, tt + 1)
                sc.activation(st[:, 5, tt:tt + 1], st[:, 4, tt:tt + 1], ACT.Sqrt).then_inc(fsd_ok, 1)

        @block.vector
        def _(dve):
            ve = nc.vector
            ch = Chain(dve, dve_step)
            dve.wait_ge(ssq_ok, TT)
            ve.tensor_scalar(st[:, 1, 0:TT], st[:, 0, 0:TT], 1.0 / D, EPS, ALU.mult, ALU.add).then_inc(rms_ok, 1)
            dve.wait_ge(std_ok, 1)
            ch.link(ve.reciprocal(st[:, 3, 0:TT], st[:, 2, 0:TT]))
            dve.wait_ge(bc_in, 16)
            for tt in range(TT):
                ve.scalar_tensor_tensor(X[:, tt, :], X[:, tt, :], st[:, 3, tt:tt + 1], bc[:, :], ALU.mult,
                                        ALU.mult).then_inc(h_ok, 1)
            for i in range(2 * TT):
                dve.wait_ge(ah_ok, i + 1)
                tt, half = i // 2, i % 2
                ks = slice(4 * half, 4 * half + 4)
                dst = actl[:, :].rearrange("p (k t) -> p k t", k=KD)[:, ks, tt * P:(tt + 1) * P]
                hi = acth[:, :].rearrange("p (k t) -> p k t", k=KD)[:, ks, tt * P:(tt + 1) * P].bitcast(F32)
                ve.tensor_tensor(dst, bank[i][:, :].rearrange("p (k t) -> p k t", k=4), hi,
                                 ALU.subtract).then_inc(al_ok, 1)
            dve.wait_ge(cols_t, 1)
            ch.link(ve.tensor_copy(cols[:, :], bank[2][:, 0:52]))
            ve.tensor_scalar(hc[:, :], cols[:, 0:40], 0.5, None, ALU.mult)
            ve.tensor_tensor(lb[:, 0, :], cols[:, 48:52], cols[:, 48:52], ALU.subtract).then_inc(hc_ok, 1)
            dve.wait_ge(act_step, 1)
            ch.link(ve.reciprocal(lb[:, 1, :], lb[:, 3, :]))
            ch.link(ve.tensor_tensor(lb[:, 2, :], lb[:, 3, :], lb[:, 1, :], ALU.mult))
            ch.link(ve.tensor_tensor(lb[:, 0, :], lb[:, 2, :], lb[:, 2, :], ALU.subtract))
            ch.link(ve.tensor_scalar(lb[:, 1, :], lb[:, 0, :], -1.0, 1.0, ALU.mult, ALU.add))
            ve.tensor_scalar(lb[:, 2, :], lb[:, 1, :], -1.0, None, ALU.mult).then_inc(hc_ok, 1)

            g = 0
            for what, n in order:
                if what == "unit":
                    kind, c = units[n]
                    for j in range(2 if kind in "fqx" else TT):
                        src = bank[g % 2]
                        if kind == "q":
                            dve.wait_ge(grp, g + 1)
                            hd = (n - U["q"][0]) * 2 + j
                            ve.tensor_copy(q[:, :, hd * P:(hd + 1) * P],
                                           src[:, :].rearrange("p (t n) -> p t n", t=TT)).then_inc(ev_dve, 1)
                        elif kind == "x":
                            jj = (n - U["x"][0]) * 2 + j
                            dve.wait_ge(grp, g + 1)
                            a = acc[:, jj % 2, :]
                            ch.link(ve.tensor_scalar(a, src[:, :], hc[:, 8 * (CONV - 1) + jj:8 * (CONV - 1) + jj + 1],
                                                     hc[:, 32 + jj:33 + jj], ALU.mult, ALU.add))
                            for k in range(CONV - 2, -1, -1):
                                s = CONV - 1 - k
                                ins = ve.scalar_tensor_tensor(a[:, s:], src[:, 0:T - s], hc[:, 8 * k + jj:8 * k + jj + 1],
                                                              a[:, s:], ALU.mult, ALU.add)
                                if k:
                                    ch.link(ins)
                            ins.then_inc(cv_acc, 1)
                            dve.wait_ge(cv_th, jj + 1)
                            if jj < 4:
                                if jj >= 2:
                                    dve.wait_ge(cv_t, jj - 1)
                                dst = cvx[:, jj % 2, :]
                            else:
                                dst = bct[:, jj - 4, :]
                            ve.scalar_tensor_tensor(dst, th, 1.0, a, ALU.add, ALU.mult).then_inc(ev_dve, 1)
                        elif kind in "gz":
                            k = (n - U["g"][0]) * TT + j
                            dve.wait_ge(gt_th, k + 1)
                            c0 = (n - U[kind][0]) * UC
                            dst = (sg if kind == "g" else sz)[:, j, c0:c0 + UC]
                            ve.scalar_tensor_tensor(dst, sq[:, 0:UC], 1.0, src[:, 0:UC], ALU.add,
                                                    ALU.mult).then_inc(ev_dve, 1)
                        g += 1
                elif what == "decay":
                    dve.wait_ge(sgm_ok, 1)
                    for hd in range(HH):
                        ins = ve.tensor_scalar(kk[:, :, hd * P:(hd + 1) * P], kk[:, :, hd * P:(hd + 1) * P],
                                               lb[:, 2, hd:hd + 1], lb[:, 1, hd:hd + 1], ALU.mult, ALU.add)
                    ch.link(ins)
                elif what == "dt":
                    dve.wait_ge(dt_mm, 1)
                    xd, ax, ex, zz, z2, pl, mx, d2 = (sm[:, j, :] for j in range(8))
                    ch.link(ve.tensor_tensor(xd.rearrange("p (t h) -> p t h", h=SH),
                                             bank[7][:, 0:TT * SH].rearrange("p (t h) -> p t h", h=SH),
                                             bc8[:, 0, :].unsqueeze(1).broadcast_to([P, TT, SH]), ALU.add))
                    ve.tensor_scalar(mx, xd, 0.0, None, ALU.max)
                    ch.link(ve.tensor_scalar(ax, xd, -1.0, None, ALU.mult))
                    ve.tensor_tensor(ax, ax, xd, ALU.max).then_inc(dt_abs, 1)
                    dve.wait_ge(dt_exp, 1)
                    ch.link(ve.tensor_scalar(d2, ex, 2.0, None, ALU.add))
                    ch.link(ve.reciprocal(z2, d2))
                    ch.link(ve.tensor_tensor(zz, ex, z2, ALU.mult))
                    ch.link(ve.tensor_tensor(z2, zz, zz, ALU.mult))
                    ch.link(ve.tensor_scalar(pl, z2, 1.0 / 15, None, ALU.mult))
                    for c in LN_TERMS:
                        ch.link(ve.scalar_tensor_tensor(pl, pl, 1.0 / c, z2, ALU.add, ALU.mult))
                    ch.link(ve.scalar_tensor_tensor(pl, pl, 1.0, zz, ALU.add, ALU.mult))
                    ch.link(ve.scalar_tensor_tensor(sm[:, 8, :], pl, 2.0, mx, ALU.mult, ALU.add))
                    ve.scalar_tensor_tensor(sm[:, 1, :].rearrange("p (t h) -> p t h", h=SH),
                                            sm[:, 8, :].rearrange("p (t h) -> p t h", h=SH), -1.0,
                                            sm[:, 9, 0:SH].unsqueeze(1).broadcast_to([P, TT, SH]), ALU.mult,
                                            ALU.mult).then_inc(dA_ok, 1)
                elif what == "cum":
                    dve.wait_ge(cum_mm, 1)
                    ve.tensor_copy(sm[:, 10, :], bank[7][:, 64:96])
                    ch.link(ve.tensor_copy(sm[:, 11, :], bank[7][:, 96:128]))
                    ve.tensor_tensor(sm[:, 14, :], sm[:, 11, :], sm[:, 10, :], ALU.subtract).then_inc(cum_ok, 1)
                    dve.wait_ge(cum_exp, 1)
                    ch.link(ve.memset(S, 0.0))
                elif what == "hg_exps":
                    i = n
                    if i == 0:
                        dve.wait_ge(const_ok, 1)
                    else:
                        dve.wait_ge(hg_sc, i)
                        ch.sync()
                    ve.tensor_tensor_scan(b32, reset[:, 0, :], lf[:, i, :], 0.0, ALU.mult, ALU.add)
                    ch.link(ve.tensor_tensor_scan(b128, reset[:, 1, :], lf[:, i, :], 0.0, ALU.mult, ALU.add))
                    bb = b32.rearrange("p (n c) -> p n c", c=BLK)
                    NB = W // BLK
                    ve.tensor_tensor(ep.rearrange("p (n c) -> p n c", c=BLK), bb,
                                     bb[:, :, BLK // 2:BLK // 2 + 1].broadcast_to([P, NB, BLK]), ALU.subtract)
                    ev, xe = h4(b32)[:, :, 0, :], h4(x32)[:, :, 0, :]
                    ve.tensor_tensor(xe, ev[:, :, BLK - 1:BLK].broadcast_to([P, NB // 2, BLK]), ev, ALU.subtract)
                    b3 = b128.rearrange("p (h t) -> p h t", h=HH)
                    ve.tensor_tensor(x64.rearrange("p (h t) -> p h t", h=HH), b3,
                                     b3[:, :, P // 2 - 1:P // 2].broadcast_to([P, HH, P]), ALU.subtract)
                    ve.tensor_tensor(ke.rearrange("p (h t) -> p h t", h=HH),
                                     b3[:, :, P - 1:P].broadcast_to([P, HH, P]), b3, ALU.subtract).then_inc(hg_sub, 1)
                    dve.wait_ge(hg_exp, i + 1)
                    ve.tensor_tensor(ep, ep, q[:, i, :], ALU.mult)
                    ve.tensor_tensor(en, en, kk[:, i, :], ALU.mult)
                    ve.tensor_tensor(h4(x32)[:, :, 0, :], h4(x32)[:, :, 0, :], h4(kk[:, i, :])[:, :, 0, :], ALU.mult)
                    ve.tensor_tensor(h4(x32)[:, :, 1, :], h4(x32)[:, :, 1, :], h4(q[:, i, :])[:, :, 1, :], ALU.mult)
                    m2 = x64.rearrange("p (h s c) -> p h s c", s=2, c=2 * BLK)
                    k2 = kk[:, i, :].rearrange("p (h s c) -> p h s c", s=2, c=2 * BLK)
                    q2 = q[:, i, :].rearrange("p (h s c) -> p h s c", s=2, c=2 * BLK)
                    ve.tensor_tensor(m2[:, :, 0, :], m2[:, :, 0, :], k2[:, :, 0, :], ALU.mult)
                    ve.tensor_tensor(m2[:, :, 1, :], m2[:, :, 1, :], q2[:, :, 1, :], ALU.mult)
                    ve.tensor_tensor(ke, ke, kk[:, i, :], ALU.mult)
                    ve.tensor_tensor(qb[:, i % 2, :], qb[:, i % 2, :], q[:, i, :], ALU.mult).then_inc(hg_ops, 1)
                elif what == "hg_scores":
                    i = n
                    dve.wait_ge(hg_sc, i + 1)
                    ve.copy_predicated(sct[:, i % 2, :].rearrange("p (h t) -> p h t", h=HH),
                                       blockm[:, :].bitcast(U32).unsqueeze(1).broadcast_to([P, HH, P]),
                                       bank[3][:, :].rearrange("p (h t) -> p h t", h=HH)).then_inc(hg_sa, 1)
                elif what == "hg_out":
                    i = n
                    dve.wait_ge(hg_sq, i + 1)
                    ve.tensor_reduce(st[:, 3, i * HH:(i + 1) * HH], sq.rearrange("p (h t) -> p h t", h=HH), AX_X,
                                     ALU.add)
                    ve.tensor_copy(X[:, i, SW:SW + HW], bank[5][:, :]).then_inc(hg_ev, 1)
                    dve.wait_ge(hg_kv, i + 1)
                    for hd in range(HH):
                        c = slice(hd * P, (hd + 1) * P)
                        ins = ve.scalar_tensor_tensor(S[:, c], S[:, c], dec[:, i % 2, hd:hd + 1], bank[6][:, c], ALU.mult,
                                                      ALU.add)
                    ins.then_inc(hg_st, 1)
                elif what == "ssd_scores":
                    i = n
                    dve.wait_ge(ss_mm, i + 1)
                    if i == 0:
                        dve.wait_ge(cv_ev, 6)
                        ch.link(ve.memset(hs, 0.0))
                    else:
                        dve.wait_ge(ss_h, i)
                        ch.sync()
                    dtv = sm[:, 8, i * SH:(i + 1) * SH]
                    for gr in range(GS):
                        cum = sm[:, 10, i * SH + gr * HPG:i * SH + (gr + 1) * HPG]
                        ins = ve.tensor_tensor(E[:, gr * 512:(gr + 1) * 512].rearrange("p (h t) -> p h t", h=HPG),
                                               bank[3 + gr][:, :].rearrange("p (h t) -> p h t", h=HPG),
                                               cum.unsqueeze(2).broadcast_to([P, HPG, P]), ALU.subtract)
                    ins.then_inc(ss_seg, 1)
                    x3 = xs[:, i, :].rearrange("p (h c) -> p h c", h=SH)
                    ch.link(ve.tensor_tensor(xdt.rearrange("p (h c) -> p h c", h=SH), x3,
                                             dtv.unsqueeze(2).broadcast_to([P, SH, SP]), ALU.mult))
                    ve.tensor_tensor(xw.rearrange("p (h c) -> p h c", h=SH), xdt.rearrange("p (h c) -> p h c", h=SH),
                                     sm[:, 14, i * SH:(i + 1) * SH].unsqueeze(2).broadcast_to([P, SH, SP]), ALU.mult)
                    dve.wait_ge(ss_exp, i + 1)
                    for gr in range(GS):
                        e3 = E[:, gr * 512:(gr + 1) * 512].rearrange("p (h t) -> p h t", h=HPG)
                        ins = ve.tensor_tensor(e3, bank[2][:, gr * P:(gr + 1) * P].unsqueeze(1).broadcast_to(
                            [P, HPG, P]), e3, ALU.mult)
                    ins.then_inc(ss_m, 1)
                elif what == "ssd_out":
                    i = n
                    dve.wait_ge(ss_y, i + 1)
                    y3 = yt.rearrange("p (h c) -> p h c", h=SH)
                    ch.link(ve.tensor_tensor(y3, xs[:, i, :].rearrange("p (h c) -> p h c", h=SH),
                                             bc8[:, 2, :].unsqueeze(2).broadcast_to([P, SH, SP]), ALU.mult))
                    yd = X[:, i, 0:SW]
                    if i == 0:
                        ve.tensor_tensor(yd, yt, bank[5][:, :], ALU.add).then_inc(ss_ev, 1)
                    else:
                        ch.link(ve.tensor_tensor(yt, yt, bank[5][:, :], ALU.add))
                        ch.link(ve.tensor_tensor(yd.rearrange("p (h c) -> p h c", h=SH),
                                                 bank[6][:, :].rearrange("p (h c) -> p h c", h=SH),
                                                 sm[:, 12, i * SH:(i + 1) * SH].unsqueeze(2).broadcast_to([P, SH, SP]),
                                                 ALU.mult))
                        ve.tensor_tensor(yd, yd, yt, ALU.add).then_inc(ss_ev, 1)
                    dve.wait_ge(ss_h, i + 1)
                    ch.link(ve.tensor_tensor(hs.rearrange("p (h c) -> p h c", h=SH),
                                             hs.rearrange("p (h c) -> p h c", h=SH),
                                             sm[:, 13, i * SH:(i + 1) * SH].unsqueeze(2).broadcast_to([P, SH, SP]),
                                             ALU.mult))
                    ve.tensor_tensor(hs, hs, bank[7][:, :], ALU.add).then_inc(hs_ok, 1)
            dve.wait_ge(hs_ok, TT)
            for tt in range(TT):
                ve.tensor_tensor(X[:, tt, 0:SW], X[:, tt, 0:SW], sz[:, tt, :], ALU.mult).then_inc(yz_ok, 1)
            dve.wait_ge(ssq_ok, TT + 1)
            ve.tensor_scalar(st[:, 4, 0:16], st[:, 3, 0:16], 1.0 / P, EPS, ALU.mult, ALU.add)
            ve.tensor_scalar(st[:, 4, 16:24], st[:, 3, 16:24], 0.25 / GW, EPS, ALU.mult, ALU.add).then_inc(rms_ok, 1)
            dve.wait_ge(std_ok, 2)
            ch.link(ve.reciprocal(st[:, 1, :], st[:, 5, :]))
            ch.link(ve.tensor_scalar(st[:, 2, :], st[:, 1, :], 0.5, None, ALU.mult))
            for tt in range(TT):
                for gr in range(GS):
                    c = slice(gr * GW, (gr + 1) * GW)
                    ve.tensor_scalar(X[:, tt, c], X[:, tt, c], st[:, 2, 16 + tt * GS + gr:17 + tt * GS + gr], None,
                                     ALU.mult)
                for hd in range(HH):
                    c = slice(SW + hd * P, SW + (hd + 1) * P)
                    ins = ve.scalar_tensor_tensor(X[:, tt, c], X[:, tt, c],
                                                  st[:, 2, tt * HH + hd:tt * HH + hd + 1],
                                                  sg[:, tt, hd * P:(hd + 1) * P], ALU.mult, ALU.mult)
                ins.then_inc(yg_ok, 1)
            for f in range(MT):
                dve.wait_ge(ah_ok, 2 * TT + f + 1)
                c = slice(f * T, (f + 1) * T)
                ve.scalar_tensor_tensor(actl[:, c], bank[f][:, :], cols[:, 40 + f:41 + f], acth[:, c].bitcast(F32),
                                        ALU.mult, ALU.subtract).then_inc(al_ok, 1)
            dve.wait_ge(xres_in, 16)
            for u in range(n_in, n_front):
                c = slice(units[u][1], units[u][1] + UC)
                for tt in range(TT):
                    dve.wait_ge(grp, g + 1)
                    ve.tensor_tensor(xres[:, tt, c], bank[g % 2][:, 0:UC], xres[:, tt, c], ALU.add).then_inc(ev_dve, 1)
                    g += 1
            dve.wait_ge(ssq_ok, 2 * TT + 1)
            ve.tensor_scalar(st[:, 4, 0:TT], st[:, 0, 0:TT], 1.0 / D, EPS, ALU.mult, ALU.add).then_inc(rms_ok, 1)
            dve.wait_ge(std_ok, 3)
            ch.link(ve.reciprocal(st[:, 1, 0:TT], st[:, 5, 0:TT]))
            dve.wait_ge(bc2_in, 16)
            for tt in range(TT):
                ve.scalar_tensor_tensor(X[:, tt, :], xres[:, tt, :], st[:, 1, tt:tt + 1], bc[:, :], ALU.mult,
                                        ALU.mult).then_inc(h2_ok, 1)
            for i in range(2 * TT):
                dve.wait_ge(h2_tr, i + 1)
                ve.tensor_copy(h2t[:, (i // 2) % 2, (i % 2) * 512:(i % 2 + 1) * 512],
                               bank[2 + i % 4][:, :]).then_inc(h2_ev, 1)
            dve.wait_ge(lg_mm, 1)
            dve.wait_ge(moe_mem, 1)
            ch.link(ve.tensor_copy(lg, bank[7][:, 0:TT * (G + NE)].rearrange("p (t n) -> p t n", t=TT)))

            def first_max(scores, top, hot, eq, w, wm):
                ch.link(ve.tensor_reduce(top, scores, AX_X, ALU.max))
                ch.link(ve.tensor_tensor(eq, scores, top.unsqueeze(2).broadcast_to([P, TT, 4]), ALU.is_equal))
                ch.link(ve.tensor_tensor(w, eq, prio.unsqueeze(1).broadcast_to([P, TT, 4]), ALU.mult))
                ch.link(ve.tensor_reduce(wm, w, AX_X, ALU.max))
                ch.link(ve.tensor_tensor(hot, w, wm.unsqueeze(2).broadcast_to([P, TT, 4]), ALU.is_equal))

            lgg = lg[:, :, 0:G]
            lge = lg[:, :, G:G + NE].rearrange("p t (g j) -> p t g j", g=G)
            ghot, hot1, hot2, ing, rest = r4[:, 4], r4[:, 5], r4[:, 6], r4[:, 7], r4[:, 8]
            first_max(lgg, r1[:, 0], ghot, r4[:, 2], r4[:, 3], r1[:, 5])
            ve.tensor_tensor(r4[:, 0], lgg, r1[:, 0].unsqueeze(2).broadcast_to([P, TT, G]),
                             ALU.subtract).then_inc(ge_in, 1)
            pick = r16[:, 0].rearrange("p t (g j) -> p t g j", g=G)
            ch.link(ve.tensor_tensor(pick, lge, ghot.unsqueeze(3).broadcast_to([P, TT, G, EG]), ALU.mult))
            ch.link(ve.tensor_reduce(ing, pick.rearrange("p t g j -> p t j g"), AX_X, ALU.add))
            first_max(ing, r1[:, 1], hot1, r4[:, 2], r4[:, 3], r1[:, 5])
            ch.link(ve.scalar_tensor_tensor(rest, hot1, NEG, ing, ALU.mult, ALU.add))
            first_max(rest, r1[:, 2], hot2, r4[:, 2], r4[:, 3], r1[:, 5])
            ve.tensor_tensor(r1[:, 3], r1[:, 2], r1[:, 1], ALU.subtract).then_inc(e2_in, 1)
            for n, hot in ((1, hot1), (2, hot2)):
                ve.tensor_tensor(r16[:, n].rearrange("p t (g j) -> p t g j", g=G),
                                 ghot.unsqueeze(3).broadcast_to([P, TT, G, EG]),
                                 hot.unsqueeze(2).broadcast_to([P, TT, G, EG]), ALU.mult)
            ch.link(ve.tensor_copy(vals[:, :, :, 0], tokc.unsqueeze(2).broadcast_to([P, TT, NE])))
            ch.link(ve.tensor_tensor(r16[:, 3], r16[:, 1], r16[:, 2], ALU.add))
            ve.tensor_copy(mb, r16[:, 3]).then_inc(m_ok, 1)
            ve.scalar_tensor_tensor(vals[:, :, :, 1], r16[:, 2], float(T), tokc.unsqueeze(2).broadcast_to([P, TT, NE]),
                                    ALU.mult, ALU.add)
            dve.wait_ge(ge_ok, 1)
            ch.link(ve.tensor_reduce(r1[:, 6], r4[:, 1], AX_X, ALU.add))
            dve.wait_ge(e2_ok, 1)
            ch.link(ve.tensor_scalar(r1[:, 7], r1[:, 4], 1.0, None, ALU.add))
            ch.link(ve.tensor_tensor(r1[:, 7], r1[:, 7], r1[:, 6], ALU.mult))
            ch.link(ve.reciprocal(r1[:, 8], r1[:, 7]))
            ve.tensor_tensor(r1[:, 9], r1[:, 8], r1[:, 4], ALU.mult)
            dve.wait_ge(pos_mm, 1)
            pos = bank[6][:, 0:TT * NE].rearrange("p (t e) -> p t e", t=TT)
            ve.scalar_tensor_tensor(r16[:, 4], pos, 1.0, r16[:, 3], ALU.add, ALU.mult)
            ch.link(ve.tensor_reduce(rnd[:, 0:1], bank[6][:, TT * NE:TT * NE + NE], AX_X, ALU.max))
            ch.link(ve.tensor_scalar(rnd[:, 1:2], rnd[:, 0:1], float(CAP), 1.0, ALU.is_gt, ALU.add))
            for k in range(2, T // CAP):
                ch.link(ve.scalar_tensor_tensor(rnd[:, 1:2], rnd[:, 0:1], float(k * CAP), rnd[:, 1:2], ALU.is_gt,
                                                ALU.add))
            ve.tensor_copy(rounds, rnd[:, 1:2]).then_inc(routed, 1)

            def slots(e, step):
                ve.tensor_copy(vale, vals[:, :, bass.ds(e, 1), :].rearrange("p t o c -> p t (o c)"))
                ve.tensor_tensor(onehot, iota1.unsqueeze(1).broadcast_to([P, TT, P]),
                                 r16[:, 4][:, :, bass.ds(e, 1)].broadcast_to([P, TT, P]),
                                 ALU.is_equal).then_inc(q_ok, 1)

            def indices(e, step, b):
                dve.wait_ge(ix_mm, step + 1)
                ve.tensor_scalar(gix[:, b:b + 1], bank[7][:, 0:1], float(NO_SLOT), None, ALU.add)
                ve.tensor_scalar(six[:, bass.ds(e, 1)], bank[7][:, 1:2], float(NO_SLOT), None,
                                 ALU.add).then_inc(ix_ok, 1)

            def rest_tokens(step, b):
                for h in range(2):
                    c = slice(h * 512, (h + 1) * 512)
                    dve.wait_ge(gh_ok, step * 2 + (h + 1))
                    ve.tensor_tensor(gtl[b][:, c], bank[2 + h][:, :], gth[b][:, c].bitcast(F32),
                                     ALU.subtract).then_inc(gl_ok, 1)

            def split_b(step, b):
                for h in range(2):
                    c = slice(h * UNIT // 2, (h + 1) * UNIT // 2)
                    dve.wait_ge(whb_ok, step * 2 + (h + 1))
                    ve.tensor_tensor(wl[:, 1, c], raw_b[b][:, c], wh[:, 1, c].bitcast(F32),
                                     ALU.subtract).then_inc(wlb_ok, 1)

            def split_c(step, b, h):
                c = slice(h * UNIT // 2, (h + 1) * UNIT // 2)
                dve.wait_ge(whc_ok, step * 2 + (h + 1))
                ve.tensor_tensor(wcl[:, c], raw_c[b][:, c], wch[:, c].bitcast(F32), ALU.subtract).then_inc(wlc_ok, 1)

            def dve_step_(e, step, b, uses, ahead1, ahead2, ahead3):
                o = 1 - b
                if ahead1:
                    rest_tokens(step + 1, o)
                if ahead2:
                    indices(e + 2, step + 2, b)
                split_c(step, b, 0)
                dve.wait_ge(sil_ok, step + 1)
                ve.tensor_tensor(hid, bank[b][:, FE:2 * FE], sil, ALU.mult).then_inc(hid_ok, 1)
                split_c(step, b, 1)
                dve.wait_ge(hh_ok, step + 1)
                ve.tensor_tensor(hidl[:, :], bank[4][:, 0:FE], hidh[:, :].bitcast(F32), ALU.subtract).then_inc(hl_ok, 1)
                if ahead1:
                    split_b(step + 1, o)
                if ahead3:
                    slots(e + 3, step + 3)
                dve.wait_ge(dn, step * 2 + 4)
                dve.wait_ge(y_free, step + 1)
                ve.tensor_copy(ysb[:, b, 512:1024], bank[6][:, :]).then_inc(y1_ok, 1)

            def dve_round(r, base):
                used = r * PAIRS
                slots(0, base)
                indices(0, base, 0)
                slots(1, base + 1)
                indices(1, base + 1, 1)
                slots(2, base + 2)
                split_b(base, 0)
                rest_tokens(base, 0)
                with dve.Fori(0, PAIRS - 2) as pp:
                    for b in range(2):
                        dve_step_(pp * 2 + b, base + pp * 2 + b, b, used + pp + 1, True, True, True)
                for e in range(NE - 4, NE):
                    dve_step_(e, base + e, e % 2, used + e // 2 + 1, e + 1 < NE, e + 2 < NE, e + 3 < NE)
                ve.tensor_scalar(iota1, iota1, float(CAP), None, ALU.add).then_inc(next_ok, 1)
                dve.wait_ge(next_ok, r + 1)

            for freed, n in AHEAD_DVE:
                dve.sem_inc(freed, n)
            expert_rounds(dve, dve_round)
            dve.wait_ge(bc3_in, 16)
            for tt in range(TT):
                dve.wait_ge(pair_in[tt], 16)
                for c in range(2):
                    ins = ve.scalar_tensor_tensor(xres[:, tt, :], pairs[:, tt, c, :], r1[:, 8 + c, tt:tt + 1],
                                                  xres[:, tt, :], ALU.mult, ALU.add)
                    if c == 0:
                        ch.link(ins)
                ins.then_inc(res_ok, 1)
                dve.wait_ge(fsq_ok, tt + 1)
                ve.tensor_scalar(st[:, 4, tt:tt + 1], st[:, 0, tt:tt + 1], 1.0 / D, EPS, ALU.mult,
                                 ALU.add).then_inc(fms_ok, 1)
                dve.wait_ge(fsd_ok, tt + 1)
                ch.link(ve.reciprocal(st[:, 1, tt:tt + 1], st[:, 5, tt:tt + 1]))
                ve.scalar_tensor_tensor(xres[:, tt, :], xres[:, tt, :], st[:, 1, tt:tt + 1], bc[:, :], ALU.mult,
                                        ALU.mult).then_inc(fin_ok, 1)

        @block.tensor
        def _(pe):
            te = nc.tensor
            ak = acth[:, :].rearrange("p (k t) -> p k t", k=KD)
            al = actl[:, :].rearrange("p (k t) -> p k t", k=KD)
            pe.wait_ge(const_ok, 1)
            for tt in range(TT):
                pe.wait_ge(h_ok, tt + 1)
                for half in range(2):
                    for k in range(4):
                        ins = te.transpose(bank[2 * tt + half][:, k * P:(k + 1) * P],
                                           X[:, tt, (4 * half + k) * P:(4 * half + k + 1) * P], ident[:, :])
                    ins.then_inc(tr_ok, 1)
            pe.wait_ge(al_ok, 3)
            pe.wait_ge(const_in, 16 * 9)
            te.transpose(bank[2][:, 0:52], rows[0:52, :], ident[0:52, 0:52]).then_inc(cols_t, 1)
            pe.wait_ge(al_ok, 2 * TT)

            def products(acc_ap, terms):
                n = len(terms)
                for j, (a, b) in enumerate(terms):
                    ins = te.matmul(acc_ap, a, b, start=(j == 0), stop=(j == n - 1))
                return ins

            def unit(u, g):
                kind, _ = units[u]
                pe.wait_ge(wl_ok, u + 1)
                uh = wh[:, u % SPL, :].rearrange("p (k n) -> p k n", k=KD)
                ul = wl[:, u % SPL, :].rearrange("p (k n) -> p k n", k=KD)
                for j in range(2 if kind in "fqx" else TT):
                    if g >= 2:
                        who, cnt = evacuated(g - 2)
                        pe.wait_ge(ev_act if who == "act" else ev_dve, cnt)
                    terms = []
                    for k in range(KD):
                        if kind in "fqx":
                            c = slice(j * P, (j + 1) * P)
                            terms += [(uh[:, k, c], ak[:, k, :]), (uh[:, k, c], al[:, k, :]), (ul[:, k, c], ak[:, k, :])]
                        else:
                            t = slice(j * P, (j + 1) * P)
                            terms += [(ak[:, k, t], uh[:, k, :]), (ak[:, k, t], ul[:, k, :]), (al[:, k, t], uh[:, k, :])]
                    dst = bank[g % 2][:, :] if kind in "fqx" else bank[g % 2][:, 0:UC]
                    products(dst, terms).then_inc(grp, 1)
                    g += 1
                return g

            g = 0
            for what, n in order:
                if what == "unit":
                    g = unit(n, g)
                elif what == "dt":
                    pe.wait_ge(dtw_l, 1)
                    dh = dtwh[:, :].rearrange("p (k n) -> p k n", k=KD)
                    dl = dtwl[:, :].rearrange("p (k n) -> p k n", k=KD)
                    for tt in range(TT):
                        t = slice(tt * P, (tt + 1) * P)
                        terms = []
                        for k in range(KD):
                            terms += [(ak[:, k, t], dh[:, k, :]), (ak[:, k, t], dl[:, k, :]), (al[:, k, t], dh[:, k, :])]
                        ins = products(bank[7][:, tt * SH:(tt + 1) * SH], terms)
                    ins.then_inc(dt_mm, 1)
                elif what == "cum":
                    pe.wait_ge(dA_ok, 1)
                    te.matmul(bank[7][:, 64:96], upto[:, :], sm[:, 1, :], start=True, stop=True)
                    te.matmul(bank[7][:, 96:128], ones[:, :], sm[:, 1, :], start=True, stop=True).then_inc(cum_mm, 1)
                elif what == "hg_scores":
                    i = n
                    pe.wait_ge(hg_ops, i + 1)
                    if i >= 1:
                        pe.wait_ge(hg_sb, i)
                    if i >= 2:
                        pe.wait_ge(cv_ev, 2 * (i - 1))
                    m2 = x64.rearrange("p (h t) -> p h t", h=HH)
                    m1 = x32.rearrange("p (h t) -> p h t", h=HH)
                    for hd in range(HH):
                        c = slice(hd * P, (hd + 1) * P)
                        te.matmul(bank[3][:, c], en[:, c], ep[:, c], start=True, stop=True)
                        te.matmul(bank[4][0:64, hd * P + 64:(hd + 1) * P], m2[:, hd, 0:64], m2[:, hd, 64:128],
                                  start=True, stop=True)
                        te.matmul(bank[4][0:32, hd * P + 32:hd * P + 64], m1[:, hd, 0:32], m1[:, hd, 32:64],
                                  start=True, stop=True)
                        te.matmul(bank[4][64:96, hd * P + 96:(hd + 1) * P], m1[:, hd, 64:96], m1[:, hd, 96:128],
                                  start=True, stop=True)
                        ins = te.transpose(bank[2][:, c], ke[:, c], ident[:, :])
                    ins.then_inc(hg_sc, 1)
                elif what == "hg_out":
                    i = n
                    pe.wait_ge(hg_sa, i + 1)
                    pe.wait_ge(hg_sb, i + 1)
                    if i >= 1:
                        pe.wait_ge(hg_st, i)
                    for hd in range(HH):
                        c = slice(hd * P, (hd + 1) * P)
                        if i >= 1:
                            te.matmul(bank[5][:, c], qb[:, i % 2, c], S[:, c], start=True, stop=False)
                        ins = te.matmul(bank[5][:, c], sct[:, i % 2, c], v[:, i, c], start=(i == 0), stop=True)
                    ins.then_inc(hg_o, 1)
                    for hd in range(HH):
                        c = slice(hd * P, (hd + 1) * P)
                        ins = te.matmul(bank[6][:, c], ket[:, c], v[:, i, c], start=True, stop=True)
                    ins.then_inc(hg_kv, 1)
                elif what == "conv_t":
                    j = n
                    if j < 4:
                        pe.wait_ge(ev_dve, evacuated(unit_end[U["x"][0] - 1] + j)[1])
                        src = cvx[:, j % 2, :]
                    else:
                        pe.wait_ge(ev_dve, evacuated(unit_end[U["x"][0] - 1] + j)[1])
                        src = bct[:, j - 4, :]
                    b = 7 if j % 2 else 2
                    if j >= 2:
                        pe.wait_ge(cv_ev, j - 1)
                    if j == 1:
                        pe.wait_ge(cum_ok, 1)
                    pe.wait_ge(hg_sb, min(TT, j // 2 + 2))
                    for tt in range(TT):
                        ins = te.transpose(bank[b][:, tt * P:(tt + 1) * P], src[:, tt * P:(tt + 1) * P], ident[:, :])
                    ins.then_inc(cv_t, 1)
                elif what == "ssd_scores":
                    i = n
                    if i == 0:
                        pe.wait_ge(hg_sa, TT)
                        pe.wait_ge(hg_sb, TT)
                        pe.wait_ge(cv_ev, 6)
                        pe.wait_ge(ev_dve, evacuated(unit_end[U["x"][-1]] - 1)[1])
                    else:
                        pe.wait_ge(ss_m, i)
                    for gr in range(GS):
                        te.matmul(bank[3 + gr][:, :], identb[:, :], negm[:, :].unsqueeze(1).broadcast_to([P, HPG, P]),
                                  start=True, stop=False, skip_group_check=True)
                        for hd in range(HPG):
                            col = i * SH + gr * HPG + hd
                            te.matmul(bank[3 + gr][:, hd * P:(hd + 1) * P],
                                      sm[:, 1, col:col + 1].broadcast_to([P, P]), upto[:, :], start=False,
                                      stop=(hd == HPG - 1), skip_group_check=True)
                    for gr in range(GS):
                        t = slice(i * P, (i + 1) * P)
                        ins = te.matmul(bank[2][:, gr * P:(gr + 1) * P], bct[:, gr, t], bct[:, GS + gr, t], start=True,
                                        stop=True)
                    ins.then_inc(ss_mm, 1)
                elif what == "ssd_out":
                    i = n
                    pe.wait_ge(ss_m, i + 1)
                    if i == 0:
                        pe.wait_ge(hg_st, TT)
                    else:
                        pe.wait_ge(ss_ev, i)
                    for hd in range(SH):
                        te.matmul(bank[5][:, hd * SP:(hd + 1) * SP], E[:, hd * P:(hd + 1) * P],
                                  xdt[:, hd * SP:(hd + 1) * SP], start=True, stop=True)
                    if i >= 1:
                        pe.wait_ge(hs_ok, i)
                    for gr in range(GS):
                        t = slice(i * P, (i + 1) * P)
                        ins = te.matmul(bank[6][:, gr * GW:(gr + 1) * GW], bct[:, GS + gr, t],
                                        hs[:, gr * GW:(gr + 1) * GW], start=True, stop=True)
                    ins.then_inc(ss_y, 1)
                    for gr in range(GS):
                        ins = te.matmul(bank[7][:, gr * GW:(gr + 1) * GW], btok[:, i, gr * P:(gr + 1) * P],
                                        xw[:, gr * GW:(gr + 1) * GW], start=True, stop=True)
                    ins.then_inc(ss_h, 1)
            pe.wait_ge(yg_ok, TT)
            for f in range(MT):
                for tt in range(TT):
                    ins = te.transpose(bank[f][:, tt * P:(tt + 1) * P], X[:, tt, f * P:(f + 1) * P], ident[:, :])
                ins.then_inc(tr_ok, 1)
            pe.wait_ge(al_ok, 2 * TT + MT)
            for u in range(n_in, n_front):
                g = unit(u, g)
            for tt in range(TT):
                pe.wait_ge(h2_ok, tt + 1)
                for half in range(2):
                    i = 2 * tt + half
                    if i >= 4:
                        pe.wait_ge(h2_ev, i - 3)
                    for k in range(4):
                        ins = te.transpose(bank[2 + i % 4][:, k * P:(k + 1) * P],
                                           X[:, tt, (4 * half + k) * P:(4 * half + k + 1) * P], ident[:, :])
                    ins.then_inc(h2_tr, 1)
                pe.wait_ge(h2_ev, 2 * tt + 2)
                if tt == 0:
                    pe.wait_ge(rt_in, 32)
                ht = h2t[:, tt % 2, :].rearrange("p (k t) -> p k t", k=KD)
                for k in range(KD):
                    ins = te.matmul(bank[7][:, tt * (G + NE):(tt + 1) * (G + NE)], ht[:, k, :], rt[:, k, :],
                                    start=(k == 0), stop=(k == KD - 1))
            ins.then_inc(lg_mm, 1)
            pe.wait_ge(m_ok, 1)
            for tt in range(TT + 1):
                dst = bank[6][:, tt * NE:(tt + 1) * NE]
                for t2 in range(tt):
                    ins = te.matmul(dst, onesb, mb[:, t2, :], start=(t2 == 0), stop=(tt == TT and t2 == TT - 1))
                if tt < TT:
                    te.matmul(dst, before, mb[:, tt, :], start=(tt == 0), stop=True)
            ins.then_inc(pos_mm, 1)

            def find_tokens(step):
                pe.wait_ge(q_ok, step + 1)
                for tt in range(TT):
                    ins = te.matmul(bank[7][:, 0:2], onehot[:, tt, :], vale[:, tt, :], start=(tt == 0), stop=(tt == TT - 1))
                ins.then_inc(ix_mm, 1)

            def turn_tokens(step, b, uses):
                pe.wait_ge(gat_in[b], uses * 16)
                pe.wait_ge(gl_ok, step * 2 + 2)
                for half in range(2):
                    for k in range(4):
                        ins = te.transpose(bank[2 + half][:, k * P:(k + 1) * P],
                                           hg[:, b, (4 * half + k) * P:(4 * half + k + 1) * P], ident[:, :])
                    ins.then_inc(g_tr, 1)

            def gate_up(b, slot, ks, first, last):
                kh = KD // 2
                uh = wh[:, slot, :].rearrange("p (k n) -> p k n", k=kh)
                ul = wl[:, slot, :].rearrange("p (k n) -> p k n", k=kh)
                for k in ks:
                    kt = slot * kh + k
                    ah, al_ = gth[b][:, kt * P:(kt + 1) * P], gtl[b][:, kt * P:(kt + 1) * P]
                    te.matmul(bank[b][:, :], ah, uh[:, k, :], start=(first and k == 0), stop=False)
                    te.matmul(bank[b][:, :], ah, ul[:, k, :], start=False, stop=False)
                    ins = te.matmul(bank[b][:, :], al_, uh[:, k, :], start=False, stop=(last and k == kh - 1))
                return ins

            def gate_up_a1(step, b):
                pe.wait_ge(gl_ok, step * 2 + 4)
                pe.wait_ge(hid_ok, step)
                pe.wait_ge(wla_ok, step * 2 + 1)
                gate_up(b, 0, (0, 1), True, False)

            def gate_up_a2(step, b):
                pe.wait_ge(wla_ok, step * 2 + 2)
                gate_up(b, 0, (2, 3), False, False).then_inc(gu_a, 1)

            def pe_step(e, step, b, uses, ahead1, ahead2):
                o = 1 - b
                if ahead1:
                    turn_tokens(step + 1, o, uses + b)
                if ahead2:
                    pe.wait_ge(ix_ok, step + 2)
                    find_tokens(step + 2)
                pe.wait_ge(wlb_ok, step * 2 + 2)
                gate_up(b, 1, range(4), False, True).then_inc(gu_b, 1)
                if ahead1:
                    gate_up_a1(step + 1, o)
                pe.wait_ge(hid_ok, step + 2)
                pe.wait_ge(hl_ok, step + 1)
                for k in range(2):
                    ins = te.transpose(bank[4][:, k * P:(k + 1) * P], hid[:, k * P:(k + 1) * P], ident[:, :])
                ins.then_inc(hid_tr, 1)
                if ahead1:
                    gate_up_a2(step + 1, o)
                pe.wait_ge(hl_ok, step + 2)
                pe.wait_ge(wlc_ok, step * 2 + 2)
                c3h = wch.rearrange("p (k n) -> p k n", k=2)
                c3l = wcl.rearrange("p (k n) -> p k n", k=2)
                for h in range(2):
                    pe.wait_ge(y0_ok if h == 0 else y1_ok, step + 1)
                    terms = []
                    for k in range(2):
                        c, n = slice(k * P, (k + 1) * P), slice(h * 512, (h + 1) * 512)
                        terms += [(hidh[:, c], c3h[:, k, n]), (hidh[:, c], c3l[:, k, n]), (hidl[:, c], c3h[:, k, n])]
                    products(bank[5 + h][:, :], terms).then_inc(dn, 1)

            def pe_round(r, base):
                used = r * PAIRS
                find_tokens(base)
                pe.wait_ge(ix_ok, base + 1)
                find_tokens(base + 1)
                turn_tokens(base, 0, used + 1)
                pe.wait_ge(gl_ok, base * 2 + 4)
                pe.wait_ge(wla_ok, base * 2 + 1)
                gate_up(0, 0, (0, 1), True, False)
                gate_up_a2(base, 0)
                with pe.Fori(0, PAIRS - 1) as pp:
                    for b in range(2):
                        pe_step(pp * 2 + b, base + pp * 2 + b, b, used + pp + 1, True, True)
                pe_step(NE - 2, base + NE - 2, 0, used + PAIRS, True, False)
                pe_step(NE - 1, base + NE - 1, 1, used + PAIRS, False, False)

            pe.sem_inc(dn, 2)
            expert_rounds(pe, pe_round)


_INS = ["x", "norm_mix_w", "w_in", "conv_w", "conv_b", "dt_bias", "a_log", "d_skip", "ssd_norm_w", "hgrn_lb_logits",
        "hgrn_norm_w", "w_out", "norm_ffn_w", "router_group", "router_expert", "w_gate", "w_up", "w_down",
        "final_norm_w"]


def kernel(**inputs):
    import numpy as np
    import concourse.bacc as bacc
    from concourse.bass_utils import run_bass_kernel_spmd

    nc = bacc.Bacc("TRN2", target_bir_lowering=False, num_devices=1, dynamic_dma_scratch_size=8192)
    arrays, args = {}, []
    for name in _INS:
        a = np.ascontiguousarray(inputs[name])
        arrays[f"in_{name}_dram"] = a
        args.append(nc.dram_tensor(f"in_{name}_dram", a.shape, mybir.dt.from_np(a.dtype), kind="ExternalInput").ap())
    shape = np.shape(inputs["x"])
    args.append(nc.dram_tensor("out_0_dram", shape, F32, kind="ExternalOutput").ap())
    trunk(nc, *args)
    r = run_bass_kernel_spmd(nc, [arrays], core_ids=[0])
    return r.results[0]["out_0_dram"]
```

```python
from contextlib import ExitStack

import concourse.bass as bass
from concourse import mybir

ALU = mybir.AluOpType
ACT = mybir.ActivationFunctionType
AX_X = mybir.AxisListType.X
F32 = mybir.dt.float32
F32R = mybir.dt.float32r
BF16 = mybir.dt.bfloat16
F16 = mybir.dt.float16
I32 = mybir.dt.int32
U32 = mybir.dt.uint32

P = 128
UNIT = 2048
EPS = 1e-6
BLK = 32
NEG = -1e30
NO_SLOT = 2048
LN_TERMS = (13, 11, 9, 7, 5, 3)


class Chain:

    def __init__(self, eng, sem):
        self.eng, self.sem, self.n = eng, sem, 0

    def mark(self, ins):
        self.n += 1
        ins.then_inc(self.sem, 1)
        return self.n

    def link(self, ins):
        self.mark(ins)
        self.eng.wait_ge(self.sem, self.n)

    def sync(self, n=None):
        self.eng.wait_ge(self.sem, self.n if n is None else n)


def trunk(nc, x, norm_mix_w, w_in, conv_w, conv_b, dt_bias, a_log, d_skip, ssd_norm_w, hgrn_lb_logits,
          hgrn_norm_w, w_out, norm_ffn_w, router_group, router_expert, w_gate, w_up, w_down, final_norm_w, out):
    _, T, D = x.shape
    TT = T // P
    KD = D // P
    CONV = conv_w.shape[1]
    SH = dt_bias.shape[1]
    SW = ssd_norm_w.shape[1]
    XBC = conv_w.shape[2]
    SP = SW // SH
    HW = hgrn_norm_w.shape[1]
    HH = HW // P
    GS = 2
    HPG = SH // GS
    GW = SW // GS
    MT = (SW + HW) // P
    G = router_group.shape[2]
    NE = w_gate.shape[1]
    EG = NE // G
    FE = w_gate.shape[3]
    assert T == 512 and D == 1024 and XBC == SW + 2 * GS * P and HPG * P == 512 and FE == 256

    UC = UNIT // KD
    cz, cx, cdt = 0, SW, SW + XBC
    cq = cdt + SH
    cf, ci, cg = cq + HW, cq + 2 * HW, cq + 3 * HW
    first = {"f": cf, "q": cq, "i": ci, "g": cg, "z": cz, "x": cx}
    units = [(kind, first[kind] + n * UC) for kind, n in
             (("f", 0), ("f", 1), ("x", 0), ("x", 1), ("q", 0), ("x", 2), ("q", 1), ("i", 0), ("i", 1), ("z", 0),
              ("x", 3), ("z", 1), ("g", 0), ("g", 1))]
    n_in = len(units)
    units += [("o", j * UC) for j in range(D // UC)]
    n_front = len(units)
    groups = []
    unit_end = []
    for kind, _ in units:
        groups += [(kind, {"f": "act", "i": "act", "x": "conv"}.get(kind, "dve"))] * 2
        unit_end.append(len(groups))

    def evacuated(g):
        who = groups[g][1]
        return who, sum(w == who for _, w in groups[:g + 1])

    n_in_groups = unit_end[n_in - 1]

    unit_no = {}
    for n, (kind, _) in enumerate(units):
        unit_no.setdefault(kind, []).append(n)

    xgroup = [sum(groups[i][0] == "x" for i in range(g)) for g in range(len(groups))]

    U = unit_no
    order = [("dt", 0), ("unit", U["f"][0]), ("dt_tokens", 0), ("unit", U["f"][1]), ("cum", 0),
             ("unit", U["x"][0]), ("decay", 0), ("unit", U["x"][1]), ("keys", 0), ("conv_t", 0), ("conv_t", 1),
             ("unit", U["q"][0]), ("hg_decays", 0), ("conv_t", 2), ("conv_t", 3), ("unit", U["x"][2]),
             ("unit", U["q"][1]),
             ("hg_operands", 0), ("conv_t", 4), ("conv_t", 5), ("unit", U["i"][0]), ("hg_scores", 0),
             ("hg_decays", 1), ("unit", U["i"][1]), ("hg_operands", 1), ("hg_out", 0), ("hg_scores", 1),
             ("hg_decays", 2), ("hg_operands", 2), ("unit", U["z"][0]), ("hg_out", 1), ("hg_scores", 2),
             ("hg_decays", 3), ("hg_operands", 3), ("unit", U["x"][3]), ("hg_out", 2), ("hg_scores", 3),
             ("unit", U["z"][1]), ("hg_out", 3), ("ssd_scores", 0), ("unit", (U["g"][0], (0,))), ("ssd_out", 0),
             ("ssd_scores", 1), ("unit", (U["g"][0], (1,))), ("ssd_out", 1), ("ssd_scores", 2),
             ("unit", (U["g"][1], (0,))), ("ssd_out", 2), ("ssd_scores", 3), ("gate", 0), ("gate", 1), ("gate", 2),
             ("unit", (U["g"][1], (1,))), ("ssd_out", 3), ("hg_norm", 0), ("gate", 3)]
    order = [(what, (n, (0, 1)) if what == "unit" and isinstance(n, int) else n) for what, n in order]

    CONSTS = 6
    RAW = 3
    SPL = 2

    with ExitStack() as ctx:
        def sb(name, shape, dt=F32):
            return ctx.enter_context(nc.sbuf_tensor(name, shape, dt))

        def sem(name):
            return ctx.enter_context(nc.semaphore(name))

        raw = sb("raw", [P, RAW, UNIT])
        wh = sb("wh", [P, SPL, UNIT], F32R)
        wl = sb("wl", [P, SPL, UNIT], F32R)
        acth = sb("acth", [P, KD * T], F32R)
        actl = sb("actl", [P, KD * T], F32R)
        bc = sb("bc", [P, D])
        X = sb("X", [P, TT, D])
        arena = sb("arena", [P, 23552])
        ident = sb("ident", [P, P])
        identb = sb("identb", [P, P], BF16)
        ones = sb("ones", [P, P])
        upto = sb("upto", [P, P])
        negm = sb("negm", [P, P], BF16)
        blockm = sb("blockm", [P, P])
        rows = sb("rows", [P, P])
        cols = sb("cols", [P, 44])
        hc = sb("hc", [P, 40])
        lb = sb("lb", [P, 4, HH])
        bc8 = sb("bc8", [P, 3, SH])
        dtw = sb("dtw", [P, KD * SH])
        dtwh = sb("dtwh", [P, KD * SH], F32R)
        dtwl = sb("dtwl", [P, KD * SH], F32R)
        sm = sb("sm", [P, 16, TT * SH])
        st = sb("st", [P, 6, 24])
        dec = sb("dec", [P, 2, HH])
        hidh = sb("hidh", [P, FE], F32R)
        hidl = sb("hidl", [P, FE], F32R)
        eps = sb("eps", [P, 2])
        gate = sb("gate", [P, 2, 2 * UC])
        rt = sb("rt", [P, KD, G + NE])
        reset = sb("reset", [P, 2, T], BF16)

        ofs = [0]

        def part(n):
            a = ofs[0]
            ofs[0] += n
            return arena[:, a:a + n]

        W = HH * P
        q = part(TT * W).rearrange("p (t n) -> p t n", t=TT)
        lf = part(TT * W).rearrange("p (t n) -> p t n", t=TT)
        kk = part(TT * W).rearrange("p (t n) -> p t n", t=TT)
        v = part(TT * HW).rearrange("p (t n) -> p t n", t=TT)
        xs = part(TT * SW).rearrange("p (t n) -> p t n", t=TT)
        bct = part(4 * T).rearrange("p (j n) -> p j n", j=4)
        btok = part(TT * GS * P).rearrange("p (t n) -> p t n", t=TT)
        conv0 = ofs[0]
        cvx = part(2 * T).rearrange("p (b n) -> p b n", b=2)
        acc = part(2 * T).rearrange("p (b n) -> p b n", b=2)
        yt = part(T)
        hg0 = ofs[0]
        b32, b128, ep, en, x32, x64, ke = (part(W) for _ in range(7))
        qb = part(2 * W).rearrange("p (b n) -> p b n", b=2)
        sct = part(2 * W).rearrange("p (b n) -> p b n", b=2)
        ket = part(W)
        S = part(W)
        sq = part(W)
        hs = part(SW)
        assert ofs[0] <= 23552
        gsq = arena[:, hg0:hg0 + 4 * W]
        E = arena[:, conv0:conv0 + SH * P]
        xdt = arena[:, conv0 + 1024:conv0 + 1536]
        xw = arena[:, conv0 + 1536:conv0 + 2048]
        sg = q
        sz = X[:, :, 0:SW]
        xres = arena[:, TT * D:2 * TT * D].rearrange("p (t n) -> p t n", t=TT)

        ofs[0] = 0
        raw_a = [raw[:, 0, :], raw[:, 1, :]]
        raw_b = [raw[:, 2, :], part(UNIT)]
        raw_c = [part(UNIT)]
        ofs[0] = 2 * TT * D
        raw_c += [part(UNIT)]
        hg = part(2 * D).rearrange("p (b n) -> p b n", b=2)
        ysb = part(2 * D).rearrange("p (b n) -> p b n", b=2)
        h2t = part(2 * D).rearrange("p (b n) -> p b n", b=2)
        onehot = part(TT * P // 2).bitcast(F16).rearrange("p (t s) -> p t s", t=TT)
        vals = part(TT * NE).bitcast(F16).rearrange("p (t e c) -> p t e c", t=TT, c=2)
        vale = part(TT).bitcast(F16).rearrange("p (t c) -> p t c", t=TT)
        sil = part(FE)
        hid = part(FE)
        iota1 = part(P)
        iotai = part(P).bitcast(I32)
        tokc = part(TT)
        prio = part(EG)
        lg = part(TT * (G + NE)).rearrange("p (t n) -> p t n", t=TT)
        lgf = h2t[0:G + NE, 0, 0:T]
        r4 = part(12 * TT * 4).rearrange("p (i t n) -> p i t n", i=12, t=TT)
        r1 = part(12 * TT).rearrange("p (i t) -> p i t", i=12)
        r16 = part(5 * TT * NE).rearrange("p (i t n) -> p i t n", i=5, t=TT)
        mb = part(TT * NE // 2).bitcast(BF16).rearrange("p (t n) -> p t n", t=TT)
        before = part(P // 2).bitcast(BF16)
        onesb = part(P // 2).bitcast(BF16)
        gix = part(2).bitcast(I32)
        six = part(NE).bitcast(I32)
        sixe = part(2).bitcast(I32)
        rnd = part(4)
        rounds = part(1).bitcast(I32)
        pairs = [arena[:, a:a + 2 * D].rearrange("p (c n) -> p c n", c=2) for a in (0, 2 * D, 8 * D, 10 * D)]
        assert ofs[0] <= 23552
        wch, wcl = acth[:, 0:UNIT], actl[:, 0:UNIT]
        gth = [acth[:, UNIT + b * D:UNIT + (b + 1) * D] for b in range(2)]
        gtl = [actl[:, UNIT + b * D:UNIT + (b + 1) * D] for b in range(2)]

        bank = [ctx.enter_context(nc.psum_tensor(f"bank{i}", [P, 512], F32)) for i in range(8)]

        x_in = [sem(f"x_in{i}") for i in range(TT)]
        bc_in = sem("bc_in")
        const_in = sem("const_in")
        dtw_in = sem("dtw_in")
        raw_in = [sem(f"raw_in{i}") for i in range(RAW)]
        xres_in = sem("xres_in")
        out_st = sem("out_st")

        pool_step = sem("pool_step")
        dve_step = sem("dve_step")
        act_step = sem("act_step")
        const_ok = sem("const_ok")
        std_ok = sem("std_ok")
        h_ok = sem("h_ok")
        tr_ok = sem("tr_ok")
        ah_ok = sem("ah_ok")
        al_ok = sem("al_ok")
        cols_t = sem("cols_t")
        hc_ok = sem("hc_ok")
        wh_ok = sem("wh_ok")
        wl_ok = sem("wl_ok")
        grp = sem("grp")
        ev_act = sem("ev_act")
        ev_dve = sem("ev_dve")
        sgm_ok = sem("sgm_ok")
        dtw_h = sem("dtw_h")
        dtw_l = sem("dtw_l")
        dt_f = sem("dt_f")
        dt_c = sem("dt_c")
        dt_mm = sem("dt_mm")
        dt_abs = sem("dt_abs")
        dt_exp = sem("dt_exp")
        dA_ok = sem("dA_ok")
        cum_mm = sem("cum_mm")
        cum_ok = sem("cum_ok")
        cum_exp = sem("cum_exp")
        hg_sub = sem("hg_sub")
        hg_exp = sem("hg_exp")
        hg_ops = sem("hg_ops")
        hg_sc = sem("hg_sc")
        hg_sa = sem("hg_sa")
        hg_sb = sem("hg_sb")
        hg_o = sem("hg_o")
        hg_kv = sem("hg_kv")
        hg_sq = sem("hg_sq")
        hg_ev = sem("hg_ev")
        hg_st = sem("hg_st")
        cv_acc = sem("cv_acc")
        cv_th = sem("cv_th")
        cv_ok = sem("cv_ok")
        cv_t = sem("cv_t")
        cv_ev = sem("cv_ev")
        gt_th = sem("gt_th")
        ss_mm = sem("ss_mm")
        ss_seg = sem("ss_seg")
        ss_exp = sem("ss_exp")
        ss_m = sem("ss_m")
        ss_y = sem("ss_y")
        ss_h = sem("ss_h")
        ss_ev = sem("ss_ev")
        hs_ok = sem("hs_ok")
        yz_ok = sem("yz_ok")
        yg_ok = sem("yg_ok")
        mixw_in = sem("mixw_in")
        gw_ok = sem("gw_ok")
        h2_evb = sem("h2_evb")
        lg_t = sem("lg_t")
        eps_ok = sem("eps_ok")
        lb_exp = sem("lb_exp")
        lg_c = sem("lg_c")
        bc2_in = sem("bc2_in")
        bc3_in = sem("bc3_in")
        h2_st = sem("h2_st")
        rt_in = sem("rt_in")
        moe_mem = sem("moe_mem")
        h2_ok = sem("h2_ok")
        h2_tr = sem("h2_tr")
        h2_ev = sem("h2_ev")
        lg_mm = sem("lg_mm")
        ge_in = sem("ge_in")
        ge_ok = sem("ge_ok")
        e2_in = sem("e2_in")
        e2_ok = sem("e2_ok")
        m_ok = sem("m_ok")
        pos_mm = sem("pos_mm")
        routed = sem("routed")
        y_free = sem("y_free")
        q_ok = sem("q_ok")
        ix_mm = sem("ix_mm")
        ix_ok = sem("ix_ok")
        g_tr = sem("g_tr")
        gh_ok = sem("gh_ok")
        gl_ok = sem("gl_ok")
        wha_ok = sem("wha_ok")
        whb_ok = sem("whb_ok")
        whc_ok = sem("whc_ok")
        wla_ok = sem("wla_ok")
        wlb_ok = sem("wlb_ok")
        wlc_ok = sem("wlc_ok")
        gu_a = sem("gu_a")
        gu_b = sem("gu_b")
        sil_ok = sem("sil_ok")
        hid_ok = sem("hid_ok")
        hid_tr = sem("hid_tr")
        hh_ok = sem("hh_ok")
        hl_ok = sem("hl_ok")
        dn = sem("dn")
        y0_ok = sem("y0_ok")
        y1_ok = sem("y1_ok")
        next_ok = sem("next_ok")
        six_ok = sem("six_ok")
        pool_tick = sem("pool_tick")
        res_ok = sem("res_ok")
        fsd_ok = sem("fsd_ok")
        fin_ok = sem("fin_ok")
        ra_in, rb_in, rc_in, gat_in, sca_out = ([sem(f"{n}{b}") for b in range(2)]
                                                for n in ("ra_in", "rb_in", "rc_in", "gat_in", "sca_out"))
        pair_in = [[sem(f"pair_in{t}_{c}") for c in range(2)] for t in range(TT)]

        h2_dram = nc.dram_tensor("h2_dram", (T, D), F32, kind="Internal").ap()
        pairs_dram = nc.dram_tensor("pairs_dram", (2 * T, D), F32, kind="Internal").ap()
        AHEAD_DVE = ((gl_ok, 2), (hl_ok, 1), (hid_ok, 1), (y1_ok, 1))
        PAIRS = NE // 2
        CAP = 112
        MOST = (T + CAP - 1) // CAP

        def expert_rounds(eng, body):
            eng.wait_ge(routed, 1)
            n = eng.value_load(rounds[0:1, 0:1], min_val=1, max_val=MOST)
            with eng.Fori(0, n) as r:
                body(r, r * NE)
            return n

        def front_src(u):
            kind, c = units[u]
            w = w_out if kind == "o" else w_in
            return w[0, :, c:c + UC].rearrange("(k p) n -> p k n", p=P)

        def raw3(slot):
            return raw[:, slot, :].rearrange("p (k n) -> p k n", k=KD)

        block = ctx.enter_context(nc.Block())

        @block.sync
        def _(sp):
            for tt in range(TT):
                sp.dma_start(X[:, tt, :], x[0, tt * P:(tt + 1) * P, :]).then_inc(x_in[tt], 16)
                if tt == 1:
                    sp.dma_start(bc[:, :], norm_mix_w[0:1, :].broadcast_to([P, D])).then_inc(bc_in, 16)
            sp.dma_start(dtw[:, :].rearrange("p (k n) -> p k n", k=KD),
                         w_in[0, :, cdt:cdt + SH].rearrange("(k p) n -> p k n", p=P)).then_inc(dtw_in, 16)
            sp.dma_start(raw3(0), front_src(0)).then_inc(raw_in[0], 16)
            n = 0
            for dst, src in (
                (rows[0:32, :], conv_w[0].rearrange("k (f p) -> (k f) p", p=P)),
                (rows[32:40, :], conv_b[0].rearrange("(f p) -> f p", p=P)),
                (rows[40:44, :], hgrn_lb_logits[0].rearrange("(f p) -> f p", p=P)),
                (bc8[:, 0, :], dt_bias[0:1, :].broadcast_to([P, SH])),
                (bc8[:, 1, :], a_log[0:1, :].broadcast_to([P, SH])),
                (bc8[:, 2, :], d_skip[0:1, :].broadcast_to([P, SH])),
            ):
                sp.dma_start(dst, src).then_inc(const_in, 16)
                n += 1
            assert n == CONSTS
            for u in range(1, n_front):
                if u == RAW:
                    sp.wait_ge(h_ok, TT)
                    sp.dma_start(bc[:, 0:SW], ssd_norm_w[0:1, :].broadcast_to([P, SW])).then_inc(mixw_in, 16)
                    sp.dma_start(bc[:, SW:SW + HW], hgrn_norm_w[0:1, :].broadcast_to([P, HW])).then_inc(mixw_in, 16)
                if u >= RAW:
                    sp.wait_ge(wl_ok, u - RAW + 1)
                sp.dma_start(raw3(u % RAW), front_src(u)).then_inc(raw_in[u % RAW], 16)
            sp.wait_ge(hg_ev, TT)
            sp.dma_start(xres, x[0].rearrange("(t p) n -> p t n", p=P)).then_inc(xres_in, 16)
            sp.wait_ge(yg_ok, TT)
            sp.dma_start(bc[:, :], norm_ffn_w[0:1, :].broadcast_to([P, D])).then_inc(bc2_in, 16)
            sp.dma_start(rt[:, :, 0:G], router_group[0].rearrange("(k p) n -> p k n", p=P)).then_inc(rt_in, 16)
            sp.dma_start(rt[:, :, G:G + NE], router_expert[0].rearrange("(k p) n -> p k n", p=P)).then_inc(rt_in, 16)

            def load_expert(e, b, step):
                kh = KD // 2
                for h, (dst, into, split) in enumerate(((raw_a[b], ra_in[b], wla_ok), (raw_b[b], rb_in[b], wlb_ok))):
                    if step is not None:
                        sp.wait_ge(split, (step - 1) * 2)
                    d3 = dst.rearrange("p (k n) -> p k n", k=kh)
                    for n, w in enumerate((w_gate, w_up)):
                        src = w[0, bass.ds(e, 1), h * kh * P:(h + 1) * kh * P, :]
                        sp.dma_start(d3[:, :, n * FE:(n + 1) * FE],
                                     src.rearrange("o (k p) f -> p (o k) f", p=P)).then_inc(into, 16)
                if step is not None:
                    sp.wait_ge(wlc_ok, (step - 1) * 2)
                src = w_down[0, bass.ds(e, 1), :, :].rearrange("o (k p) d -> p (o k) d", p=P)
                sp.dma_start(raw_c[b].rearrange("p (k n) -> p k n", k=FE // P), src).then_inc(rc_in[b], 16)

            sp.wait_ge(wl_ok, n_front)
            load_expert(0, 0, None)
            load_expert(1, 1, None)
            with sp.Fori(1, PAIRS) as pp:
                for b in range(2):
                    load_expert(pp * 2 + b, b, pp * 2 + b)
            sp.wait_ge(h2_ok, TT)
            sp.dma_start(bc[:, :], final_norm_w[None, :].broadcast_to([P, D])).then_inc(bc3_in, 16)
            sp.wait_ge(routed, 1)
            n = sp.value_load(rounds[0:1, 0:1], min_val=1, max_val=MOST)
            with sp.If(n > 1):
                with sp.Fori(1, n) as r:
                    with sp.Fori(0, PAIRS) as pp:
                        for b in range(2):
                            load_expert(pp * 2 + b, b, r * NE + pp * 2 + b)
            for b in range(2):
                sp.wait_ge(sca_out[b], n * (16 * PAIRS))
            for tt in range(TT):
                for c in range(2):
                    sp.dma_start(pairs[tt][:, c, :], pairs_dram[c * T + tt * P:c * T + (tt + 1) * P, :])\
                        .then_inc(pair_in[tt][c], 16)
            for tt in range(TT):
                sp.wait_ge(fin_ok, tt + 1)
                sp.dma_start(out[0, tt * P:(tt + 1) * P, :], xres[:, tt, :]).then_inc(out_st, 16)
            sp.wait_ge(out_st, 16 * TT)

        @block.gpsimd
        def _(pool):
            ch = Chain(pool, pool_step)
            gp = nc.gpsimd
            gp.memset(eps[:, 0:1], EPS)
            gp.memset(eps[:, 1:2], 4 * EPS).then_inc(eps_ok, 1)
            gp.memset(ident[:, :], 0.0)
            gp.memset(identb[:, :], 0.0)
            gp.memset(ones[:, :], 1.0)
            gp.memset(upto[:, :], 1.0)
            gp.memset(negm[:, :], 0.0)
            gp.memset(reset[:, :, :], 1.0)
            ch.link(gp.memset(blockm[:, :], 1.0))
            for m in (ident, identb):
                gp.affine_select(out=m[:, :], in_=m[:, :], compare_op=ALU.not_equal, fill=1.0, base=0,
                                 pattern=[[-1, P]], channel_multiplier=1)
            gp.affine_select(out=upto[:, :], in_=upto[:, :], compare_op=ALU.is_ge, fill=0.0, base=0,
                             pattern=[[1, P]], channel_multiplier=-1)
            gp.affine_select(out=negm[:, :], in_=negm[:, :], compare_op=ALU.is_ge, fill=NEG, base=0,
                             pattern=[[1, P]], channel_multiplier=-1)
            ch.link(gp.affine_select(out=blockm[:, :], in_=blockm[:, :], compare_op=ALU.is_ge, fill=0.0, base=0,
                                     pattern=[[1, P]], channel_multiplier=-1))
            bm = blockm[:, :].rearrange("p (n c) -> p n c", c=BLK)
            gp.affine_select(out=bm, in_=bm, compare_op=ALU.is_ge, fill=0.0, base=0,
                             pattern=[[-BLK, P // BLK], [0, BLK]], channel_multiplier=1)
            gp.memset(reset[:, 0, :].rearrange("p (n c) -> p n c", c=BLK)[:, :, 0:1], 0.0)
            gp.memset(sct[:, :, :], 0.0)
            gp.memset(reset[:, 1, :].rearrange("p (n c) -> p n c", c=P)[:, :, 0:1], 0.0).then_inc(const_ok, 1)

            pool.wait_ge(dtw_h, 1)
            gp.tensor_tensor(dtwl[:, :], dtw[:, :], dtwh[:, :].bitcast(F32), ALU.subtract).then_inc(dtw_l, 1)
            for u in range(n_front):
                if u - SPL in U["g"]:
                    n = U["g"].index(u - SPL)
                    pool.wait_ge(mixw_in, 32)
                    pool.wait_ge(ev_dve, evacuated(unit_end[u - SPL] - 1)[1])
                    c = slice(n * UC, (n + 1) * UC)
                    gp.tensor_tensor(sg[:, :, c], sg[:, :, c],
                                     bc[:, SW + n * UC:SW + (n + 1) * UC].unsqueeze(1).broadcast_to([P, TT, UC]),
                                     ALU.mult).then_inc(gw_ok, 1)
                pool.wait_ge(wh_ok, u + 1)
                gp.tensor_tensor(wl[:, u % SPL, :], raw[:, u % RAW, :], wh[:, u % SPL, :].bitcast(F32),
                                 ALU.subtract).then_inc(wl_ok, 1)
            pool.wait_ge(yg_ok, TT)
            gp.memset(hg[:, :, :], 0.0)
            gp.memset(onesb, 1.0)
            gp.memset(before, 1.0)
            for i in range(EG):
                gp.memset(prio[:, i:i + 1], float(EG - i))
            ch.link(gp.iota(iotai, [[1, P]], base=1, channel_multiplier=0))
            ch.link(gp.tensor_copy(iota1, iotai))
            ch.link(gp.iota(iotai[:, 0:TT], [[P, TT]], base=-NO_SLOT, channel_multiplier=1))
            gp.tensor_copy(tokc, iotai[:, 0:TT])
            gp.affine_select(out=before, in_=before, compare_op=ALU.is_ge, fill=0.0, base=-1, pattern=[[1, P]],
                             channel_multiplier=-1).then_inc(moe_mem, 1)

            def gather(step, b, first=False):
                pool.wait_ge(ix_ok, step + 1)
                pool.sem_inc(pool_tick, 1)
                gp.indirect_dma_start(hg[0:CAP, b, :], None, h2_dram,
                                      bass.IndirectOffsetOnAxis(ap=gix[0:CAP, b:b + 1], axis=0),
                                      bounds_check=T - 1, oob_is_err=False).then_inc(gat_in[b], 16)

            def split_a(step, b):
                for h in range(2):
                    c = slice(h * UNIT // 2, (h + 1) * UNIT // 2)
                    pool.wait_ge(wha_ok, step * 2 + (h + 1))
                    gp.tensor_tensor(wl[:, 0, c], raw_a[b][:, c], wh[:, 0, c].bitcast(F32),
                                     ALU.subtract).then_inc(wla_ok, 1)

            def scatter(e, step, b):
                pool.wait_ge(y0_ok, step + 2)
                pool.wait_ge(y1_ok, step + 2)
                pool.sem_inc(pool_tick, 1)
                gp.tensor_copy(sixe[:, b:b + 1], six[:, bass.ds(e, 1)]).then_inc(six_ok, 1)
                pool.wait_ge(six_ok, step + 1)
                pool.sem_inc(pool_tick, 1)
                gp.indirect_dma_start(pairs_dram, bass.IndirectOffsetOnAxis(ap=sixe[0:CAP, b:b + 1], axis=0),
                                      ysb[0:CAP, b, :], None, bounds_check=2 * T - 1, oob_is_err=False)\
                    .then_inc(sca_out[b], 16)

            def outputs_stored(b, uses):
                pool.wait_ge(sca_out[b], uses * 16)
                pool.sem_inc(y_free, 1)

            def pool_expert(e, step, b, uses_other, ahead2, ahead3):
                if ahead2:
                    split_a(step + 2, b)
                if ahead3:
                    gather(step + 3, 1 - b)
                if uses_other is not None:
                    outputs_stored(1 - b, uses_other)
                scatter(e, step, b)

            def pool_round(r, base):
                gather(base, 0)
                gather(base + 1, 1)
                with pool.If(r > 0):
                    split_a(base, 0)
                split_a(base + 1, 1)
                gather(base + 2, 0)
                used = r * PAIRS
                pool_expert(0, base, 0, None, True, True)
                pool_expert(1, base + 1, 1, used + 1, True, True)
                with pool.Fori(1, PAIRS - 2) as pp:
                    for b in range(2):
                        pool_expert(pp * 2 + b, base + pp * 2 + b, b, used + pp + b, True, True)
                for e in range(NE - 4, NE):
                    pool_expert(e, base + e, e % 2, used + (e + 1) // 2, e + 2 < NE, e + 3 < NE)
                outputs_stored((NE - 1) % 2, used + PAIRS)

            split_a(0, 0)
            for h in range(2):
                c = slice(h * UNIT // 2, (h + 1) * UNIT // 2)
                pool.wait_ge(whb_ok, h + 1)
                gp.tensor_tensor(wl[:, 1, c], raw_b[0][:, c], wh[:, 1, c].bitcast(F32),
                                 ALU.subtract).then_inc(wlb_ok, 1)
            pool.wait_ge(h2_st, 16 * TT)
            pool.sem_inc(y_free, 2)
            expert_rounds(pool, pool_round)

        def conv_at(jj):
            return cvx[:, jj % 2, :] if jj < 4 else bct[:, jj - 4, :]

        def h4(ap):
            return ap.rearrange("p (m s c) -> p m s c", s=2, c=BLK)

        @block.scalar
        def _(act):
            sc = nc.scalar
            ch = Chain(act, act_step)
            n_tr = [0]

            def round_unit(u):
                act.wait_ge(raw_in[u % RAW], 16 * (u // RAW + 1))
                if u >= SPL:
                    act.wait_ge(grp, unit_end[u - SPL])
                sc.activation(wh[:, u % SPL, :], raw[:, u % RAW, :], ACT.Copy).then_inc(wh_ok, 1)

            def root(dst, sums, scale, e=0):
                return sc.activation(dst, sums, ACT.Sqrt, scale=scale, bias=eps[:, e:e + 1])

            def round_turned(done, tt):
                for i in (2 * tt, 2 * tt + 1):
                    act.wait_ge(tr_ok, done + i + 1)
                    half = i % 2
                    dst = acth[:, :].rearrange("p (k t) -> p k t", k=KD)[:, 4 * half:4 * half + 4, tt * P:(tt + 1) * P]
                    sc.activation(dst, bank[i][:, :].rearrange("p (k t) -> p k t", k=4), ACT.Copy).then_inc(ah_ok, 1)

            act.wait_ge(eps_ok, 1)
            root(hidh[:, 0:1], eps[:, 0:1], 1.0)
            for tt in range(TT):
                act.wait_ge(x_in[tt], 16)
                ch.link(sc.activation(arena[:, tt * D:(tt + 1) * D], X[:, tt, :], ACT.Square,
                                      accum_out=st[:, 0, tt:tt + 1]))
                root(st[:, 2, tt:tt + 1], st[:, 0, tt:tt + 1], 1.0 / D).then_inc(std_ok, 1)
                if tt >= 2:
                    round_turned(0, tt - 2)
            act.wait_ge(dtw_in, 16)
            sc.activation(dtwh[:, :], dtw[:, :], ACT.Copy).then_inc(dtw_h, 1)
            round_turned(0, TT - 2)
            round_turned(0, TT - 1)
            round_unit(0)
            round_unit(1)
            g = gates = 0
            used_gate = []
            for what, n in order:
                if what == "unit":
                    n, parts = n
                    kind, c = units[n]
                    for j in parts:
                        t2 = slice(2 * j, 2 * j + 2)
                        if kind == "f":
                            act.wait_ge(grp, g + 1)
                            hd = U["f"].index(n) * 2 + j
                            sc.activation(kk[:, :, hd * P:(hd + 1) * P],
                                          bank[g % 2][:, :].rearrange("p (t n) -> p t n", t=TT),
                                          ACT.Sigmoid).then_inc(ev_act, 1)
                        elif kind == "i":
                            act.wait_ge(grp, g + 1)
                            c0 = U["i"].index(n) * UC
                            sc.activation(v[:, t2, c0:c0 + UC], bank[g % 2][:, :].rearrange("p (t n) -> p t n", t=2),
                                          ACT.Copy).then_inc(ev_act, 1)
                        elif kind == "x":
                            jj = xgroup[g]
                            act.wait_ge(cv_acc, jj + 1)
                            if 2 <= jj < 4:
                                act.wait_ge(cv_t, jj - 1)
                            sc.activation(conv_at(jj), acc[:, jj % 2, :], ACT.Tanh).then_inc(cv_th, 1)
                        elif kind in "gz":
                            k = gates
                            gates += 1
                            act.wait_ge(grp, g + 1)
                            if k >= 2:
                                act.wait_ge(ev_dve, used_gate[k - 2])
                            used_gate.append(evacuated(g)[1])
                            sc.activation(gate[:, k % 2, :], bank[g % 2][:, :], ACT.Tanh,
                                          scale=0.5).then_inc(gt_th, 1)
                        g += 1
                    if parts[-1] == 1 and n + SPL < n_front:
                        round_unit(n + SPL)
                elif what == "decay":
                    act.wait_ge(hc_ok, 2)
                    act.wait_ge(ev_act, 4)
                    for hd in range(HH):
                        last = sc.activation(lf[:, :, hd * P:(hd + 1) * P], kk[:, :, hd * P:(hd + 1) * P], ACT.Ln,
                                             scale=lb[:, 1, hd:hd + 1], bias=lb[:, 0, hd:hd + 1])
                    last.then_inc(sgm_ok, 1)
                elif what == "dt":
                    act.wait_ge(hc_ok, 1)
                    sc.activation(lb[:, 3, :], lb[:, 0, :], ACT.Exp).then_inc(lb_exp, 1)
                elif what == "dt_tokens":
                    act.wait_ge(dt_abs, 1)
                    sc.activation(sm[:, 9, 0:SH], bc8[:, 1, :], ACT.Exp)
                    sc.activation(sm[:, 2, :], sm[:, 1, :], ACT.Exp, scale=-1.0).then_inc(dt_exp, 1)
                elif what == "cum":
                    act.wait_ge(cum_ok, 1)
                    sc.activation(sm[:, 12, :], sm[:, 10, :], ACT.Exp)
                    sc.activation(sm[:, 13, :], sm[:, 11, :], ACT.Exp)
                    sc.activation(sm[:, 14, :], sm[:, 14, :], ACT.Exp).then_inc(cum_exp, 1)
                elif what == "hg_decays":
                    i = n
                    act.wait_ge(hg_sub, i + 1)
                    sc.activation(en, ep, ACT.Exp, scale=-1.0)
                    if i >= 2:
                        act.wait_ge(hg_kv, i - 1)
                    sc.activation(qb[:, i % 2, :], b128, ACT.Exp)
                    sc.activation(h4(x32)[:, :, 1, :], h4(b32)[:, :, 1, :], ACT.Exp)
                    sc.activation(h4(x32)[:, :, 0, :], h4(x32)[:, :, 0, :], ACT.Exp)
                    m2 = x64.rearrange("p (h s c) -> p h s c", s=2, c=2 * BLK)
                    sc.activation(m2[:, :, 0, :], m2[:, :, 0, :], ACT.Exp, scale=-1.0)
                    sc.activation(m2[:, :, 1, :], m2[:, :, 1, :], ACT.Exp)
                    if i >= 2:
                        act.wait_ge(hg_st, i - 1)
                    sc.activation(dec[:, i % 2, :], b128.rearrange("p (h t) -> p h t", h=HH)[:, :, P - 1], ACT.Exp)
                    ch.link(sc.activation(ke, ke, ACT.Exp))
                    sc.activation(ep, ep, ACT.Exp).then_inc(hg_exp, 1)
                elif what == "hg_scores":
                    i = n
                    act.wait_ge(hg_sc, i + 1)
                    act.wait_ge(hg_sa, i + 1)
                    dst = sct[:, i % 2, :].rearrange("p (h t) -> p h t", h=HH)
                    src = bank[4][:, :].rearrange("p (h t) -> p h t", h=HH)
                    sc.activation(dst[0:64, :, 64:128], src[0:64, :, 64:128], ACT.Copy)
                    sc.activation(dst[0:32, :, 32:64], src[0:32, :, 32:64], ACT.Copy)
                    sc.activation(dst[64:96, :, 96:128], src[64:96, :, 96:128], ACT.Copy)
                    sc.activation(ket, bank[2][:, :], ACT.Copy).then_inc(hg_sb, 1)
                elif what == "hg_out":
                    i = n
                    act.wait_ge(hg_o, i + 1)
                    if i >= 1:
                        act.wait_ge(hg_ev, i)
                    sc.activation(sq, bank[5][:, :], ACT.Square).then_inc(hg_sq, 1)
                elif what == "conv_t":
                    j = n
                    act.wait_ge(cv_t, j + 1)
                    src = bank[7 if j % 2 else 2][:, :].rearrange("p (t n) -> p t n", t=TT)
                    dst = xs[:, :, j * P:(j + 1) * P] if j < 4 else btok[:, :, (j - 4) * P:(j - 3) * P]
                    sc.activation(dst, src, ACT.Copy).then_inc(cv_ev, 1)
                elif what == "ssd_scores":
                    act.wait_ge(ss_seg, n + 1)
                    sc.activation(E, E, ACT.Exp).then_inc(ss_exp, 1)
                elif what == "gate":
                    if n == 0:
                        act.wait_ge(hg_exp, TT)
                    act.wait_ge(yz_ok, n + 1)
                    for gr in range(GS):
                        last = sc.activation(gsq[:, (n * GS + gr) * GW:(n * GS + gr + 1) * GW],
                                             X[:, n, gr * GW:(gr + 1) * GW], ACT.Square,
                                             accum_out=st[:, 3, 16 + n * GS + gr:17 + n * GS + gr])
                    ch.link(last)
                elif what == "hg_norm":
                    act.wait_ge(hg_ev, TT)
                    root(st[:, 5, 0:16], st[:, 3, 0:16], 4.0 / P, 1).then_inc(std_ok, 1)
            root(st[:, 5, 16:24], st[:, 3, 16:24], 1.0 / GW, 1).then_inc(std_ok, 1)
            for tt in range(TT):
                round_turned(2 * TT, tt)
            for u in range(n_in, n_front):
                if u + SPL < n_front:
                    round_unit(u + SPL)
            def turned_half(tt):
                act.wait_ge(h2_tr, 2 * tt + 2)
                act.wait_ge(lg_t, tt - 1)
                sc.activation(h2t[:, tt % 2, 512:1024], bank[3 + 2 * (tt % 2)][:, :], ACT.Copy).then_inc(h2_evb, 1)

            def store_normed(tt):
                act.wait_ge(h2_ok, tt + 1)
                act.dma_start(h2_dram[tt * P:(tt + 1) * P, :], X[:, tt, :]).then_inc(h2_st, 16)

            for t in range(0, TT, 2):
                act.wait_ge(ev_dve, evacuated(len(groups) - 2 + t // 2)[1])
                for tt in (t, t + 1):
                    last = sc.activation(X[:, tt, :], xres[:, tt, :], ACT.Square, accum_out=st[:, 0, tt:tt + 1])
                ch.link(last)
                root(st[:, 5, t:t + 2], st[:, 0, t:t + 2], 1.0 / D).then_inc(std_ok, 1)
            store_normed(0)
            store_normed(1)
            store_normed(TT - 2)
            store_normed(TT - 1)
            turned_half(2)
            turned_half(3)

            def halves(which):
                return [slice(h * UNIT // 2, (h + 1) * UNIT // 2) for h in which]

            def round_a(step, b, uses):
                act.wait_ge(ra_in[b], uses * 32)
                for c in halves((0, 1)):
                    sc.activation(wh[:, 0, c], raw_a[b][:, c], ACT.Copy).then_inc(wha_ok, 1)

            def round_b(step, b, uses, which=(0, 1)):
                act.wait_ge(rb_in[b], uses * 32)
                for c in halves(which):
                    sc.activation(wh[:, 1, c], raw_b[b][:, c], ACT.Copy).then_inc(whb_ok, 1)

            def round_c(step, b, uses):
                act.wait_ge(dn, step * 2 + 2)
                act.wait_ge(rc_in[b], uses * 16)
                for c in halves((0, 1)):
                    sc.activation(wch[:, c], raw_c[b][:, c], ACT.Copy).then_inc(whc_ok, 1)

            round_a(0, 0, 1)
            round_b(0, 0, 1)
            round_c(0, 0, 1)
            act.wait_ge(ge_in, 1)
            sc.activation(r4[:, 1], r4[:, 0], ACT.Exp).then_inc(ge_ok, 1)
            act.wait_ge(e2_in, 1)
            sc.activation(r1[:, 4], r1[:, 3], ACT.Exp).then_inc(e2_ok, 1)
            ch.link(sc.activation(dec[:, 0, 0:1], ident[:, 0:1], ACT.Silu))

            def round_tokens(step, b):
                for h in range(2):
                    act.wait_ge(g_tr, step * 2 + (h + 1))
                    sc.activation(gth[b][:, h * 512:(h + 1) * 512], bank[2 + h][:, :], ACT.Copy).then_inc(gh_ok, 1)

            def act_expert(e, step, b, uses, ahead1, ahead2, down=True):
                o = 1 - b
                uses1 = uses + b
                if ahead1:
                    round_tokens(step + 1, o)
                if down:
                    round_c(step, b, uses)
                act.wait_ge(gu_b, step + 1)
                sc.activation(sil, bank[b][:, 0:FE], ACT.Silu).then_inc(sil_ok, 1)
                if ahead1:
                    round_b(step + 1, o, uses1, (0,))
                act.wait_ge(hid_tr, step + 1)
                sc.activation(hidh[:, :], bank[4][:, 0:FE], ACT.Copy).then_inc(hh_ok, 1)
                if ahead1:
                    round_b(step + 1, o, uses1, (1,))
                if ahead2:
                    act.wait_ge(gu_a, step + 2)
                    round_a(step + 2, b, uses + 1)
                act.wait_ge(dn, step * 2 + 3)
                act.wait_ge(y_free, step + 1)
                sc.activation(ysb[:, b, 0:512], bank[5][:, :], ACT.Copy).then_inc(y0_ok, 1)

            def act_round(r, base):
                used = r * PAIRS
                with act.If(r > 0):
                    round_a(base, 0, used + 1)
                    round_b(base, 0, used + 1)
                    round_c(base, 0, used + 1)
                round_tokens(base, 0)
                act.wait_ge(gu_a, base + 1)
                round_a(base + 1, 1, used + 1)
                act_expert(0, base, 0, used + 1, True, True, down=False)
                act_expert(1, base + 1, 1, used + 1, True, True)
                with act.Fori(1, PAIRS - 1) as pp:
                    for b in range(2):
                        act_expert(pp * 2 + b, base + pp * 2 + b, b, used + pp + 1, True, True)
                act_expert(NE - 2, base + NE - 2, 0, used + PAIRS, True, False)
                act_expert(NE - 1, base + NE - 1, 1, used + PAIRS, False, False)

            act.sem_inc(y0_ok, 1)
            expert_rounds(act, act_round)
            ch.link(sc.activation(dec[:, 0, 0:1], ident[:, 0:1], ACT.Sqrt))
            for tt in range(TT):
                act.wait_ge(res_ok, tt + 1)
                ch.link(sc.activation(X[:, tt, :], xres[:, tt, :], ACT.Square, accum_out=st[:, 0, tt:tt + 1]))
                root(st[:, 5, tt:tt + 1], st[:, 0, tt:tt + 1], 1.0 / D).then_inc(fsd_ok, 1)

        @block.vector
        def _(dve):
            ve = nc.vector
            ch = Chain(dve, dve_step)
            def rest_turned(done, tt):
                for i in (2 * tt, 2 * tt + 1):
                    dve.wait_ge(ah_ok, done + i + 1)
                    half = i % 2
                    ks = slice(4 * half, 4 * half + 4)
                    dst = actl[:, :].rearrange("p (k t) -> p k t", k=KD)[:, ks, tt * P:(tt + 1) * P]
                    hi = acth[:, :].rearrange("p (k t) -> p k t", k=KD)[:, ks, tt * P:(tt + 1) * P].bitcast(F32)
                    ve.tensor_tensor(dst, bank[i][:, :].rearrange("p (k t) -> p k t", k=4), hi,
                                     ALU.subtract).then_inc(al_ok, 1)

            def hg_normed(tt):
                for hd in range(HH):
                    c = slice(SW + hd * P, SW + (hd + 1) * P)
                    ve.scalar_tensor_tensor(X[:, tt, c], X[:, tt, c], st[:, 1, tt * HH + hd:tt * HH + hd + 1],
                                            sg[:, tt, hd * P:(hd + 1) * P], ALU.mult, ALU.mult)

            for tt in range(TT):
                t1 = slice(tt, tt + 1)
                dve.wait_ge(std_ok, tt + 1)
                ch.link(ve.reciprocal(st[:, 3, t1], st[:, 2, t1]))
                if tt == 0:
                    dve.wait_ge(bc_in, 16)
                ve.scalar_tensor_tensor(X[:, tt, :], X[:, tt, :], st[:, 3, t1], bc[:, :], ALU.mult,
                                        ALU.mult).then_inc(h_ok, 1)
                if tt >= 2:
                    rest_turned(0, tt - 2)
            rest_turned(0, TT - 2)
            rest_turned(0, TT - 1)
            g = gates = 0
            for what, n in order:
                if what == "unit":
                    n, parts = n
                    kind, c = units[n]
                    for j in parts:
                        src = bank[g % 2]
                        two = src[:, :].rearrange("p (t n) -> p t n", t=2)
                        t2 = slice(2 * j, 2 * j + 2)
                        if kind == "q":
                            dve.wait_ge(grp, g + 1)
                            hd = U["q"].index(n) * 2 + j
                            ve.tensor_copy(q[:, :, hd * P:(hd + 1) * P],
                                           src[:, :].rearrange("p (t n) -> p t n", t=TT)).then_inc(ev_dve, 1)
                        elif kind == "x":
                            jj = xgroup[g]
                            dve.wait_ge(grp, g + 1)
                            a = acc[:, jj % 2, :]
                            if jj >= 2:
                                dve.wait_ge(cv_ok, jj - 1)
                            ch.link(ve.tensor_scalar(a, src[:, :], hc[:, 8 * (CONV - 1) + jj:8 * (CONV - 1) + jj + 1],
                                                     hc[:, 32 + jj:33 + jj], ALU.mult, ALU.add))
                            for k in range(CONV - 2, -1, -1):
                                s = CONV - 1 - k
                                tap = hc[:, 8 * k + jj:8 * k + jj + 1]
                                ins = ve.scalar_tensor_tensor(a[:, s:], src[:, 0:T - s], tap, a[:, s:], ALU.mult,
                                                              ALU.add)
                                if k:
                                    ch.link(ins)
                            ins.then_inc(cv_acc, 1)
                        elif kind in "gz":
                            gates += 1
                            dve.wait_ge(gt_th, gates)
                            c0 = U[kind].index(n) * UC
                            dst = (sg if kind == "g" else sz)[:, t2, c0:c0 + UC]
                            tanh = gate[:, (gates - 1) % 2, :].rearrange("p (t n) -> p t n", t=2)
                            ve.scalar_tensor_tensor(dst, tanh, 1.0, two, ALU.add, ALU.mult).then_inc(ev_dve, 1)
                        g += 1
                    if kind == "x":
                        for jj in (xgroup[g - 2], xgroup[g - 1]):
                            dve.wait_ge(cv_th, jj + 1)
                            ve.scalar_tensor_tensor(conv_at(jj), conv_at(jj), 1.0, acc[:, jj % 2, :], ALU.add,
                                                    ALU.mult).then_inc(cv_ok, 1)
                elif what == "keys":
                    dve.wait_ge(sgm_ok, 1)
                    for hd in range(HH):
                        ins = ve.tensor_scalar(kk[:, :, hd * P:(hd + 1) * P], kk[:, :, hd * P:(hd + 1) * P],
                                               lb[:, 2, hd:hd + 1], lb[:, 1, hd:hd + 1], ALU.mult, ALU.add)
                    ch.link(ins)
                elif what == "dt":
                    dve.wait_ge(dt_f, 1)
                    ve.tensor_copy(sq[0:SH, :], bank[7][0:SH, :]).then_inc(dt_c, 1)
                    dve.wait_ge(cols_t, 1)
                    ch.link(ve.tensor_copy(cols[:, :], bank[2][:, 0:44]))
                    ve.tensor_scalar(hc[:, :], cols[:, 0:40], 0.5, None, ALU.mult)
                    ve.tensor_tensor(lb[:, 0, :], cols[:, 40:44], cols[:, 40:44], ALU.subtract).then_inc(hc_ok, 1)
                    dve.wait_ge(lb_exp, 1)
                    ch.link(ve.reciprocal(lb[:, 1, :], lb[:, 3, :]))
                    ch.link(ve.tensor_tensor(lb[:, 2, :], lb[:, 3, :], lb[:, 1, :], ALU.mult))
                    ch.link(ve.tensor_tensor(lb[:, 0, :], lb[:, 2, :], lb[:, 2, :], ALU.subtract))
                    ch.link(ve.tensor_scalar(lb[:, 1, :], lb[:, 0, :], -1.0, 1.0, ALU.mult, ALU.add))
                    ve.tensor_scalar(lb[:, 2, :], lb[:, 1, :], -1.0, None, ALU.mult).then_inc(hc_ok, 1)
                elif what == "dt_tokens":
                    dve.wait_ge(dt_mm, 1)
                    xd, ax, ex, zz, z2, pl, mx, d2 = (sm[:, j, :] for j in range(8))
                    ch.link(ve.tensor_tensor(xd.rearrange("p (t h) -> p t h", h=SH),
                                             bank[7][:, 0:TT * SH].rearrange("p (t h) -> p t h", h=SH),
                                             bc8[:, 0, :].unsqueeze(1).broadcast_to([P, TT, SH]), ALU.add))
                    ve.tensor_scalar(mx, xd, 0.0, None, ALU.max)
                    ch.link(ve.tensor_scalar(ax, xd, -1.0, None, ALU.mult))
                    ve.tensor_tensor(ax, ax, xd, ALU.max).then_inc(dt_abs, 1)
                    dve.wait_ge(dt_exp, 1)
                    ch.link(ve.tensor_scalar(d2, ex, 2.0, None, ALU.add))
                    ch.link(ve.reciprocal(z2, d2))
                    ch.link(ve.tensor_tensor(zz, ex, z2, ALU.mult))
                    ch.link(ve.tensor_tensor(z2, zz, zz, ALU.mult))
                    ch.link(ve.tensor_scalar(pl, z2, 1.0 / 15, None, ALU.mult))
                    for c in LN_TERMS:
                        ch.link(ve.scalar_tensor_tensor(pl, pl, 1.0 / c, z2, ALU.add, ALU.mult))
                    ch.link(ve.scalar_tensor_tensor(pl, pl, 1.0, zz, ALU.add, ALU.mult))
                    ch.link(ve.scalar_tensor_tensor(sm[:, 8, :], pl, 2.0, mx, ALU.mult, ALU.add))
                    ve.scalar_tensor_tensor(sm[:, 1, :].rearrange("p (t h) -> p t h", h=SH),
                                            sm[:, 8, :].rearrange("p (t h) -> p t h", h=SH), -1.0,
                                            sm[:, 9, 0:SH].unsqueeze(1).broadcast_to([P, TT, SH]), ALU.mult,
                                            ALU.mult).then_inc(dA_ok, 1)
                elif what == "cum":
                    dve.wait_ge(cum_mm, 1)
                    ve.tensor_copy(sm[:, 10, :], bank[7][:, 64:96])
                    ch.link(ve.tensor_copy(sm[:, 11, :], bank[7][:, 96:128]))
                    ve.tensor_tensor(sm[:, 14, :], sm[:, 11, :], sm[:, 10, :], ALU.subtract).then_inc(cum_ok, 1)
                    dve.wait_ge(cum_exp, 1)
                    ch.link(ve.memset(S, 0.0))
                elif what == "hg_decays":
                    i = n
                    if i == 0:
                        dve.wait_ge(const_ok, 1)
                    else:
                        dve.wait_ge(hg_sc, i)
                        ch.sync()
                    ve.tensor_tensor_scan(b32, reset[:, 0, :], lf[:, i, :], 0.0, ALU.mult, ALU.add)
                    ch.link(ve.tensor_tensor_scan(b128, reset[:, 1, :], lf[:, i, :], 0.0, ALU.mult, ALU.add))
                    bb = b32.rearrange("p (n c) -> p n c", c=BLK)
                    NB = W // BLK
                    ve.tensor_tensor(ep.rearrange("p (n c) -> p n c", c=BLK), bb,
                                     bb[:, :, BLK // 2:BLK // 2 + 1].broadcast_to([P, NB, BLK]), ALU.subtract)
                    ev, xe = h4(b32)[:, :, 0, :], h4(x32)[:, :, 0, :]
                    ve.tensor_tensor(xe, ev[:, :, BLK - 1:BLK].broadcast_to([P, NB // 2, BLK]), ev, ALU.subtract)
                    b3 = b128.rearrange("p (h t) -> p h t", h=HH)
                    ve.tensor_tensor(x64.rearrange("p (h t) -> p h t", h=HH), b3,
                                     b3[:, :, P // 2 - 1:P // 2].broadcast_to([P, HH, P]), ALU.subtract)
                    ve.tensor_tensor(ke.rearrange("p (h t) -> p h t", h=HH),
                                     b3[:, :, P - 1:P].broadcast_to([P, HH, P]), b3, ALU.subtract).then_inc(hg_sub, 1)
                elif what == "hg_operands":
                    i = n
                    if i == 0:
                        dve.wait_ge(ev_dve, evacuated(unit_end[U["q"][1]] - 1)[1])
                    dve.wait_ge(hg_exp, i + 1)
                    ve.tensor_tensor(ep, ep, q[:, i, :], ALU.mult)
                    ve.tensor_tensor(en, en, kk[:, i, :], ALU.mult)
                    ve.tensor_tensor(h4(x32)[:, :, 0, :], h4(x32)[:, :, 0, :], h4(kk[:, i, :])[:, :, 0, :], ALU.mult)
                    ve.tensor_tensor(h4(x32)[:, :, 1, :], h4(x32)[:, :, 1, :], h4(q[:, i, :])[:, :, 1, :], ALU.mult)
                    m2 = x64.rearrange("p (h s c) -> p h s c", s=2, c=2 * BLK)
                    k2 = kk[:, i, :].rearrange("p (h s c) -> p h s c", s=2, c=2 * BLK)
                    q2 = q[:, i, :].rearrange("p (h s c) -> p h s c", s=2, c=2 * BLK)
                    ve.tensor_tensor(m2[:, :, 0, :], m2[:, :, 0, :], k2[:, :, 0, :], ALU.mult)
                    ve.tensor_tensor(m2[:, :, 1, :], m2[:, :, 1, :], q2[:, :, 1, :], ALU.mult)
                    ve.tensor_tensor(ke, ke, kk[:, i, :], ALU.mult)
                    ve.tensor_tensor(qb[:, i % 2, :], qb[:, i % 2, :], q[:, i, :], ALU.mult).then_inc(hg_ops, 1)
                elif what == "hg_scores":
                    i = n
                    dve.wait_ge(hg_sc, i + 1)
                    ve.copy_predicated(sct[:, i % 2, :].rearrange("p (h t) -> p h t", h=HH),
                                       blockm[:, :].bitcast(U32).unsqueeze(1).broadcast_to([P, HH, P]),
                                       bank[3][:, :].rearrange("p (h t) -> p h t", h=HH)).then_inc(hg_sa, 1)
                elif what == "hg_out":
                    i = n
                    dve.wait_ge(hg_sq, i + 1)
                    ve.tensor_reduce(st[:, 3, i * HH:(i + 1) * HH], sq.rearrange("p (h t) -> p h t", h=HH), AX_X,
                                     ALU.add)
                    ve.tensor_copy(X[:, i, SW:SW + HW], bank[5][:, :]).then_inc(hg_ev, 1)
                    if i + 1 < TT:
                        dve.wait_ge(hg_kv, i + 1)
                        for hd in range(HH):
                            c = slice(hd * P, (hd + 1) * P)
                            ins = ve.scalar_tensor_tensor(S[:, c], S[:, c], dec[:, i % 2, hd:hd + 1], bank[6][:, c],
                                                          ALU.mult, ALU.add)
                        ins.then_inc(hg_st, 1)
                elif what == "ssd_scores":
                    i = n
                    dve.wait_ge(ss_mm, i + 1)
                    if i == 0:
                        dve.wait_ge(cv_ev, 6)
                        ch.link(ve.memset(hs, 0.0))
                    else:
                        dve.wait_ge(ss_h, i)
                        ch.sync()
                    dtv = sm[:, 8, i * SH:(i + 1) * SH]
                    for gr in range(GS):
                        cum = sm[:, 10, i * SH + gr * HPG:i * SH + (gr + 1) * HPG]
                        ins = ve.tensor_tensor(E[:, gr * 512:(gr + 1) * 512].rearrange("p (h t) -> p h t", h=HPG),
                                               bank[3 + gr][:, :].rearrange("p (h t) -> p h t", h=HPG),
                                               cum.unsqueeze(2).broadcast_to([P, HPG, P]), ALU.subtract)
                    ins.then_inc(ss_seg, 1)
                    x3 = xs[:, i, :].rearrange("p (h c) -> p h c", h=SH)
                    ch.link(ve.tensor_tensor(xdt.rearrange("p (h c) -> p h c", h=SH), x3,
                                             dtv.unsqueeze(2).broadcast_to([P, SH, SP]), ALU.mult))
                    ve.tensor_tensor(xw.rearrange("p (h c) -> p h c", h=SH), xdt.rearrange("p (h c) -> p h c", h=SH),
                                     sm[:, 14, i * SH:(i + 1) * SH].unsqueeze(2).broadcast_to([P, SH, SP]), ALU.mult)
                    dve.wait_ge(ss_exp, i + 1)
                    for gr in range(GS):
                        e3 = E[:, gr * 512:(gr + 1) * 512].rearrange("p (h t) -> p h t", h=HPG)
                        ins = ve.tensor_tensor(e3, bank[2][:, gr * P:(gr + 1) * P].unsqueeze(1).broadcast_to(
                            [P, HPG, P]), e3, ALU.mult)
                    ins.then_inc(ss_m, 1)
                elif what == "ssd_out":
                    i = n
                    if i == 0:
                        dve.wait_ge(ev_dve, evacuated(unit_end[U["z"][1]] - 1)[1])
                    else:
                        dve.wait_ge(yz_ok, i)
                    y3 = yt.rearrange("p (h c) -> p h c", h=SH)
                    ch.link(ve.tensor_tensor(y3, xs[:, i, :].rearrange("p (h c) -> p h c", h=SH),
                                             bc8[:, 2, :].unsqueeze(2).broadcast_to([P, SH, SP]), ALU.mult))
                    dve.wait_ge(ss_y, i + 1)
                    ins = ve.tensor_tensor(yt, yt, bank[5][:, :], ALU.add)
                    if i:
                        ch.link(ins)
                        ve.tensor_tensor(xdt.rearrange("p (h c) -> p h c", h=SH),
                                         bank[6][:, :].rearrange("p (h c) -> p h c", h=SH),
                                         sm[:, 12, i * SH:(i + 1) * SH].unsqueeze(2).broadcast_to([P, SH, SP]),
                                         ALU.mult).then_inc(ss_ev, 1)
                        dve.wait_ge(ss_ev, i + 1)
                        ch.link(ve.tensor_tensor(yt, yt, xdt, ALU.add))
                    else:
                        ins.then_inc(ss_ev, 1)
                        dve.wait_ge(ss_ev, 1)
                    ve.tensor_tensor(sz[:, i, :], sz[:, i, :], yt, ALU.mult).then_inc(yz_ok, 1)
                    if i + 1 < TT:
                        dve.wait_ge(ss_h, i + 1)
                        ch.link(ve.tensor_tensor(hs.rearrange("p (h c) -> p h c", h=SH),
                                                 hs.rearrange("p (h c) -> p h c", h=SH),
                                                 sm[:, 13, i * SH:(i + 1) * SH].unsqueeze(2).broadcast_to([P, SH, SP]),
                                                 ALU.mult))
                        ve.tensor_tensor(hs, hs, bank[7][:, :], ALU.add).then_inc(hs_ok, 1)
                elif what == "hg_norm":
                    dve.wait_ge(std_ok, TT + 1)
                    ch.link(ve.reciprocal(st[:, 1, 0:16], st[:, 5, 0:16]))
                    dve.wait_ge(gw_ok, 2)
                    hg_normed(0)
            dve.wait_ge(std_ok, TT + 2)
            ch.link(ve.reciprocal(st[:, 1, 16:24], st[:, 5, 16:24]))
            for tt in range(TT):
                if tt:
                    hg_normed(tt)
                for gr in range(GS):
                    c = slice(gr * GW, (gr + 1) * GW)
                    ins = ve.scalar_tensor_tensor(X[:, tt, c], X[:, tt, c],
                                                  st[:, 1, 16 + tt * GS + gr:17 + tt * GS + gr],
                                                  bc[:, c], ALU.mult, ALU.mult)
                ins.then_inc(yg_ok, 1)
                if tt:
                    rest_turned(2 * TT, tt - 1)
            rest_turned(2 * TT, TT - 1)

            def turned(tt):
                dve.wait_ge(h2_tr, 2 * tt + 1)
                if tt >= 2:
                    dve.wait_ge(lg_t, tt - 1)
                ins = ve.tensor_copy(h2t[:, tt % 2, 0:512], bank[2 + 2 * (tt % 2)][:, :])
                if tt < 2:
                    dve.wait_ge(h2_tr, 2 * tt + 2)
                    ins = ve.tensor_copy(h2t[:, tt % 2, 512:1024], bank[3 + 2 * (tt % 2)][:, :])
                ins.then_inc(h2_ev, 1)

            def ffn_norm(t):
                dve.wait_ge(std_ok, TT + 3 + t // 2)
                ch.link(ve.reciprocal(st[:, 1, t:t + 2], st[:, 5, t:t + 2]))
                if t == 0:
                    dve.wait_ge(bc2_in, 16)
                for tt in (t, t + 1):
                    ve.scalar_tensor_tensor(X[:, tt, :], xres[:, tt, :], st[:, 1, tt:tt + 1], bc[:, :], ALU.mult,
                                            ALU.mult).then_inc(h2_ok, 1)

            dve.wait_ge(xres_in, 16)
            for u in range(n_in, n_front):
                c = slice(units[u][1], units[u][1] + UC)
                for t in range(0, TT, 2):
                    dve.wait_ge(grp, g + 1)
                    ve.tensor_tensor(xres[:, t:t + 2, c], bank[g % 2][:, :].rearrange("p (t n) -> p t n", t=2),
                                     xres[:, t:t + 2, c], ALU.add).then_inc(ev_dve, 1)
                    g += 1
                    if u == n_front - 1:
                        if t:
                            turned(0)
                            turned(1)
                        ffn_norm(t)
            turned(2)
            turned(3)
            dve.wait_ge(lg_t, TT)
            ve.tensor_copy(lgf, bank[7][0:G + NE, :]).then_inc(lg_c, 1)
            dve.wait_ge(lg_mm, 1)
            dve.wait_ge(moe_mem, 1)
            ch.link(ve.tensor_copy(lg, bank[6][:, 0:TT * (G + NE)].rearrange("p (t n) -> p t n", t=TT)))

            def first_max(scores, top, hot, eq, w, wm):
                ch.link(ve.tensor_reduce(top, scores, AX_X, ALU.max))
                ch.link(ve.tensor_tensor(eq, scores, top.unsqueeze(2).broadcast_to([P, TT, 4]), ALU.is_equal))
                ch.link(ve.tensor_tensor(w, eq, prio.unsqueeze(1).broadcast_to([P, TT, 4]), ALU.mult))
                ch.link(ve.tensor_reduce(wm, w, AX_X, ALU.max))
                ch.link(ve.tensor_tensor(hot, w, wm.unsqueeze(2).broadcast_to([P, TT, 4]), ALU.is_equal))

            lgg = lg[:, :, 0:G]
            lge = lg[:, :, G:G + NE].rearrange("p t (g j) -> p t g j", g=G)
            ghot, hot1, hot2, ing, rest = r4[:, 4], r4[:, 5], r4[:, 6], r4[:, 7], r4[:, 8]
            first_max(lgg, r1[:, 0], ghot, r4[:, 2], r4[:, 3], r1[:, 5])
            ve.tensor_tensor(r4[:, 0], lgg, r1[:, 0].unsqueeze(2).broadcast_to([P, TT, G]),
                             ALU.subtract).then_inc(ge_in, 1)
            pick = r16[:, 0].rearrange("p t (g j) -> p t g j", g=G)
            ch.link(ve.tensor_tensor(pick, lge, ghot.unsqueeze(3).broadcast_to([P, TT, G, EG]), ALU.mult))
            ch.link(ve.tensor_reduce(ing, pick.rearrange("p t g j -> p t j g"), AX_X, ALU.add))
            first_max(ing, r1[:, 1], hot1, r4[:, 2], r4[:, 3], r1[:, 5])
            ch.link(ve.scalar_tensor_tensor(rest, hot1, NEG, ing, ALU.mult, ALU.add))
            first_max(rest, r1[:, 2], hot2, r4[:, 2], r4[:, 3], r1[:, 5])
            ve.tensor_tensor(r1[:, 3], r1[:, 2], r1[:, 1], ALU.subtract).then_inc(e2_in, 1)
            for n, hot in ((1, hot1), (2, hot2)):
                ve.tensor_tensor(r16[:, n].rearrange("p t (g j) -> p t g j", g=G),
                                 ghot.unsqueeze(3).broadcast_to([P, TT, G, EG]),
                                 hot.unsqueeze(2).broadcast_to([P, TT, G, EG]), ALU.mult)
            ch.link(ve.tensor_copy(vals[:, :, :, 0], tokc.unsqueeze(2).broadcast_to([P, TT, NE])))
            ch.link(ve.tensor_tensor(r16[:, 3], r16[:, 1], r16[:, 2], ALU.add))
            ve.tensor_copy(mb, r16[:, 3]).then_inc(m_ok, 1)
            ve.scalar_tensor_tensor(vals[:, :, :, 1], r16[:, 2], float(T), tokc.unsqueeze(2).broadcast_to([P, TT, NE]),
                                    ALU.mult, ALU.add)
            dve.wait_ge(pos_mm, 1)
            pos = bank[6][:, 0:TT * NE].rearrange("p (t e) -> p t e", t=TT)
            ve.scalar_tensor_tensor(r16[:, 4], pos, 1.0, r16[:, 3], ALU.add, ALU.mult)
            ch.link(ve.tensor_reduce(rnd[:, 0:1], bank[6][:, TT * NE:TT * NE + NE], AX_X, ALU.max))
            ch.link(ve.tensor_scalar(rnd[:, 1:2], rnd[:, 0:1], float(CAP), 1.0, ALU.is_gt, ALU.add))
            for k in range(2, MOST):
                ch.link(ve.scalar_tensor_tensor(rnd[:, 1:2], rnd[:, 0:1], float(k * CAP), rnd[:, 1:2], ALU.is_gt,
                                                ALU.add))
            ve.tensor_copy(rounds, rnd[:, 1:2]).then_inc(routed, 1)

            def slots(e, step):
                ve.tensor_copy(vale, vals[:, :, bass.ds(e, 1), :].rearrange("p t o c -> p t (o c)"))
                ve.tensor_tensor(onehot, iota1.unsqueeze(1).broadcast_to([P, TT, P]),
                                 r16[:, 4][:, :, bass.ds(e, 1)].broadcast_to([P, TT, P]),
                                 ALU.is_equal).then_inc(q_ok, 1)

            def indices(e, step, b):
                dve.wait_ge(ix_mm, step + 1)
                ve.tensor_scalar(gix[:, b:b + 1], bank[7][:, 0:1], float(NO_SLOT), None, ALU.add)
                ve.tensor_scalar(six[:, bass.ds(e, 1)], bank[7][:, 1:2], float(NO_SLOT), None,
                                 ALU.add).then_inc(ix_ok, 1)

            def rest_tokens(step, b):
                for h in range(2):
                    c = slice(h * 512, (h + 1) * 512)
                    dve.wait_ge(gh_ok, step * 2 + (h + 1))
                    ve.tensor_tensor(gtl[b][:, c], bank[2 + h][:, :], gth[b][:, c].bitcast(F32),
                                     ALU.subtract).then_inc(gl_ok, 1)

            def split_b(step, b):
                for h in range(2):
                    c = slice(h * UNIT // 2, (h + 1) * UNIT // 2)
                    dve.wait_ge(whb_ok, step * 2 + (h + 1))
                    ve.tensor_tensor(wl[:, 1, c], raw_b[b][:, c], wh[:, 1, c].bitcast(F32),
                                     ALU.subtract).then_inc(wlb_ok, 1)

            def split_c(step, b, h):
                c = slice(h * UNIT // 2, (h + 1) * UNIT // 2)
                dve.wait_ge(whc_ok, step * 2 + (h + 1))
                ve.tensor_tensor(wcl[:, c], raw_c[b][:, c], wch[:, c].bitcast(F32), ALU.subtract).then_inc(wlc_ok, 1)

            def dve_expert(e, step, b, uses, ahead1, ahead2, ahead3, down=True):
                o = 1 - b
                if ahead1:
                    rest_tokens(step + 1, o)
                if ahead2:
                    indices(e + 2, step + 2, b)
                if down:
                    split_c(step, b, 0)
                dve.wait_ge(sil_ok, step + 1)
                ve.tensor_tensor(hid, bank[b][:, FE:2 * FE], sil, ALU.mult).then_inc(hid_ok, 1)
                if down:
                    split_c(step, b, 1)
                dve.wait_ge(hh_ok, step + 1)
                ve.tensor_tensor(hidl[:, :], bank[4][:, 0:FE], hidh[:, :].bitcast(F32), ALU.subtract).then_inc(hl_ok, 1)
                if ahead1:
                    split_b(step + 1, o)
                if ahead3:
                    slots(e + 3, step + 3)
                dve.wait_ge(dn, step * 2 + 4)
                dve.wait_ge(y_free, step + 1)
                ve.tensor_copy(ysb[:, b, 512:1024], bank[6][:, :]).then_inc(y1_ok, 1)

            def dve_round(r, base):
                used = r * PAIRS
                slots(0, base)
                indices(0, base, 0)
                slots(1, base + 1)
                indices(1, base + 1, 1)
                slots(2, base + 2)
                split_c(base, 0, 0)
                split_c(base, 0, 1)
                with dve.If(r > 0):
                    split_b(base, 0)
                rest_tokens(base, 0)
                dve_expert(0, base, 0, used + 1, True, True, True, down=False)
                dve_expert(1, base + 1, 1, used + 1, True, True, True)
                with dve.Fori(1, PAIRS - 2) as pp:
                    for b in range(2):
                        dve_expert(pp * 2 + b, base + pp * 2 + b, b, used + pp + 1, True, True, True)
                for e in range(NE - 4, NE):
                    dve_expert(e, base + e, e % 2, used + e // 2 + 1, e + 1 < NE, e + 2 < NE, e + 3 < NE)
                ve.tensor_scalar(iota1, iota1, float(CAP), None, ALU.add).then_inc(next_ok, 1)
                dve.wait_ge(next_ok, r + 1)

            for freed, n in AHEAD_DVE:
                dve.sem_inc(freed, n)
            expert_rounds(dve, dve_round)
            dve.wait_ge(ge_ok, 1)
            ch.link(ve.tensor_reduce(r1[:, 6], r4[:, 1], AX_X, ALU.add))
            dve.wait_ge(e2_ok, 1)
            ch.link(ve.tensor_scalar(r1[:, 7], r1[:, 4], 1.0, None, ALU.add))
            ch.link(ve.tensor_tensor(r1[:, 7], r1[:, 7], r1[:, 6], ALU.mult))
            ch.link(ve.reciprocal(r1[:, 8], r1[:, 7]))
            ch.link(ve.tensor_tensor(r1[:, 9], r1[:, 8], r1[:, 4], ALU.mult))
            dve.wait_ge(bc3_in, 16)
            def add_pairs(tt):
                for c in range(2):
                    dve.wait_ge(pair_in[tt][c], 16)
                    ins = ve.scalar_tensor_tensor(xres[:, tt, :], pairs[tt][:, c, :], r1[:, 8 + c, tt:tt + 1],
                                                  xres[:, tt, :], ALU.mult, ALU.add)
                    if c == 0:
                        ch.link(ins)
                ins.then_inc(res_ok, 1)

            def final_norm(tt):
                dve.wait_ge(fsd_ok, tt + 1)
                ch.link(ve.reciprocal(st[:, 1, tt:tt + 1], st[:, 5, tt:tt + 1]))
                ve.scalar_tensor_tensor(xres[:, tt, :], xres[:, tt, :], st[:, 1, tt:tt + 1], bc[:, :], ALU.mult,
                                        ALU.mult).then_inc(fin_ok, 1)

            add_pairs(0)
            for tt in range(1, TT):
                add_pairs(tt)
                final_norm(tt - 1)
            final_norm(TT - 1)

        @block.tensor
        def _(pe):
            te = nc.tensor
            ak = acth[:, :].rearrange("p (k t) -> p k t", k=KD)
            al = actl[:, :].rearrange("p (k t) -> p k t", k=KD)

            def keep_warm(n):
                for _ in range(n):
                    te.matmul(bank[1][:, 0:P], ones[:, :], upto[:, :], start=True, stop=True)

            pe.wait_ge(const_ok, 1)
            for tt in range(TT):
                pe.wait_ge(h_ok, tt + 1)
                for half in range(2):
                    for k in range(4):
                        ins = te.transpose(bank[2 * tt + half][:, k * P:(k + 1) * P],
                                           X[:, tt, (4 * half + k) * P:(4 * half + k + 1) * P], ident[:, :])
                    ins.then_inc(tr_ok, 1)
            pe.wait_ge(al_ok, 2 * TT)

            def products(acc_ap, terms):
                n = len(terms)
                for j, (a, b) in enumerate(terms):
                    ins = te.matmul(acc_ap, a, b, start=(j == 0), stop=(j == n - 1))
                return ins

            def turn_mixed(tt):
                pe.wait_ge(yg_ok, tt + 1)
                for half in range(2):
                    for k in range(4):
                        ins = te.transpose(bank[2 * tt + half][:, k * P:(k + 1) * P],
                                           X[:, tt, (4 * half + k) * P:(4 * half + k + 1) * P], ident[:, :])
                    ins.then_inc(tr_ok, 1)

            def unit(u, g, parts=(0, 1)):
                kind, _ = units[u]
                if u == n_in:
                    turn_mixed(0)
                pe.wait_ge(wl_ok, u + 1)
                uh = wh[:, u % SPL, :].rearrange("p (k n) -> p k n", k=KD)
                ul = wl[:, u % SPL, :].rearrange("p (k n) -> p k n", k=KD)
                for j in parts:
                    if g >= 2:
                        who, cnt = evacuated(g - 2)
                        pe.wait_ge({"act": ev_act, "dve": ev_dve, "conv": cv_acc}[who], cnt)
                    if kind in "fqx":
                        c = slice(j * P, (j + 1) * P)
                        terms = []
                        for k in range(KD):
                            terms += [(uh[:, k, c], ak[:, k, :]), (uh[:, k, c], al[:, k, :]),
                                      (ul[:, k, c], ak[:, k, :])]
                        ins = products(bank[g % 2][:, :], terms)
                    else:
                        for h in range(2):
                            tt = 2 * j + h
                            t = slice(tt * P, (tt + 1) * P)
                            if u == n_in:
                                if tt + 1 < TT:
                                    turn_mixed(tt + 1)
                                pe.wait_ge(al_ok, 2 * TT + 2 * tt + 2)
                            terms = []
                            for k in range(KD):
                                terms += [(ak[:, k, t], uh[:, k, :]), (ak[:, k, t], ul[:, k, :]),
                                          (al[:, k, t], uh[:, k, :])]
                            ins = products(bank[g % 2][:, h * UC:(h + 1) * UC], terms)
                    ins.then_inc(grp, 1)
                    g += 1
                return g

            def constant_columns():
                pe.wait_ge(const_in, 16 * CONSTS)
                te.transpose(bank[2][:, 0:44], rows[0:44, :], ident[0:44, 0:44]).then_inc(cols_t, 1)

            g = 0
            scored = turned = 0
            for what, n in order:
                if what == "unit":
                    g = unit(n[0], g, n[1])
                elif what == "dt":
                    pe.wait_ge(dtw_l, 1)
                    dh = dtwh[:, :].rearrange("p (k n) -> p k n", k=KD)
                    dl = dtwl[:, :].rearrange("p (k n) -> p k n", k=KD)
                    terms = []
                    for k in range(KD):
                        terms += [(dh[:, k, :], ak[:, k, :]), (dh[:, k, :], al[:, k, :]), (dl[:, k, :], ak[:, k, :])]
                    products(bank[7][0:SH, :], terms).then_inc(dt_f, 1)
                    constant_columns()
                elif what == "dt_tokens":
                    pe.wait_ge(dt_c, 1)
                    for tt in range(TT):
                        ins = te.transpose(bank[7][:, tt * SH:(tt + 1) * SH], sq[0:SH, tt * P:(tt + 1) * P],
                                           ident[0:SH, 0:SH])
                    ins.then_inc(dt_mm, 1)
                elif what == "cum":
                    pe.wait_ge(dA_ok, 1)
                    te.matmul(bank[7][:, 64:96], upto[:, :], sm[:, 1, :], start=True, stop=True)
                    te.matmul(bank[7][:, 96:128], ones[:, :], sm[:, 1, :], start=True, stop=True).then_inc(cum_mm, 1)
                elif what == "hg_scores":
                    i = n
                    pe.wait_ge(hg_ops, i + 1)
                    if i >= 1:
                        pe.wait_ge(hg_sb, i)
                    if turned:
                        pe.wait_ge(cv_ev, (turned - 1) // 2 * 2 + 1)
                    scored += 1
                    m2 = x64.rearrange("p (h t) -> p h t", h=HH)
                    m1 = x32.rearrange("p (h t) -> p h t", h=HH)
                    for hd in range(HH):
                        c = slice(hd * P, (hd + 1) * P)
                        te.matmul(bank[3][:, c], en[:, c], ep[:, c], start=True, stop=True)
                        te.matmul(bank[4][0:64, hd * P + 64:(hd + 1) * P], m2[:, hd, 0:64], m2[:, hd, 64:128],
                                  start=True, stop=True)
                        te.matmul(bank[4][0:32, hd * P + 32:hd * P + 64], m1[:, hd, 0:32], m1[:, hd, 32:64],
                                  start=True, stop=True)
                        te.matmul(bank[4][64:96, hd * P + 96:(hd + 1) * P], m1[:, hd, 64:96], m1[:, hd, 96:128],
                                  start=True, stop=True)
                        ins = te.transpose(bank[2][:, c], ke[:, c], ident[:, :])
                    ins.then_inc(hg_sc, 1)
                elif what == "hg_out":
                    i = n
                    if i == 0:
                        pe.wait_ge(ev_act, evacuated(unit_end[U["i"][1]] - 1)[1])
                    pe.wait_ge(hg_sa, i + 1)
                    pe.wait_ge(hg_sb, i + 1)
                    if i >= 1:
                        pe.wait_ge(hg_st, i)
                    for hd in range(HH):
                        c = slice(hd * P, (hd + 1) * P)
                        if i >= 1:
                            te.matmul(bank[5][:, c], qb[:, i % 2, c], S[:, c], start=True, stop=False)
                        ins = te.matmul(bank[5][:, c], sct[:, i % 2, c], v[:, i, c], start=(i == 0), stop=True)
                    ins.then_inc(hg_o, 1)
                    for hd in range(HH if i + 1 < TT else 0):
                        c = slice(hd * P, (hd + 1) * P)
                        ins = te.matmul(bank[6][:, c], ket[:, c], v[:, i, c], start=True, stop=True)
                    if i + 1 < TT:
                        ins.then_inc(hg_kv, 1)
                elif what == "conv_t":
                    j = n
                    pe.wait_ge(cv_ok, j + 1)
                    src = conv_at(j)
                    b = 7 if j % 2 else 2
                    if j >= 2:
                        pe.wait_ge(cv_ev, j - 1)
                    if j == 1:
                        pe.wait_ge(cum_ok, 1)
                    if b == 2 and scored:
                        pe.wait_ge(hg_sb, scored)
                    turned += 1
                    for tt in range(TT):
                        ins = te.transpose(bank[b][:, tt * P:(tt + 1) * P], src[:, tt * P:(tt + 1) * P], ident[:, :])
                    ins.then_inc(cv_t, 1)
                elif what == "ssd_scores":
                    i = n
                    if i == 0:
                        pe.wait_ge(hg_sa, TT)
                        pe.wait_ge(hg_sb, TT)
                        pe.wait_ge(cv_ev, 6)
                        pe.wait_ge(cv_ok, XBC // P)
                    else:
                        pe.wait_ge(ss_m, i)
                    for gr in range(GS):
                        te.matmul(bank[3 + gr][:, :], identb[:, :], negm[:, :].unsqueeze(1).broadcast_to([P, HPG, P]),
                                  start=True, stop=False, skip_group_check=True)
                        for hd in range(HPG):
                            col = i * SH + gr * HPG + hd
                            te.matmul(bank[3 + gr][:, hd * P:(hd + 1) * P],
                                      sm[:, 1, col:col + 1].broadcast_to([P, P]), upto[:, :], start=False,
                                      stop=(hd == HPG - 1), skip_group_check=True)
                    for gr in range(GS):
                        t = slice(i * P, (i + 1) * P)
                        ins = te.matmul(bank[2][:, gr * P:(gr + 1) * P], bct[:, gr, t], bct[:, GS + gr, t], start=True,
                                        stop=True)
                    ins.then_inc(ss_mm, 1)
                elif what == "ssd_out":
                    i = n
                    pe.wait_ge(ss_m, i + 1)
                    if i == 0:
                        pe.wait_ge(hg_ev, TT)
                    else:
                        pe.wait_ge(ss_ev, i)
                    for hd in range(SH):
                        ins = te.matmul(bank[5][:, hd * SP:(hd + 1) * SP], E[:, hd * P:(hd + 1) * P],
                                  xdt[:, hd * SP:(hd + 1) * SP], start=True, stop=True)
                    if i >= 1:
                        pe.wait_ge(hs_ok, i)
                    for gr in range(GS if i else 0):
                        t = slice(i * P, (i + 1) * P)
                        ins = te.matmul(bank[6][:, gr * GW:(gr + 1) * GW], bct[:, GS + gr, t],
                                        hs[:, gr * GW:(gr + 1) * GW], start=True, stop=True)
                    ins.then_inc(ss_y, 1)
                    for gr in range(GS if i + 1 < TT else 0):
                        ins = te.matmul(bank[7][:, gr * GW:(gr + 1) * GW], btok[:, i, gr * P:(gr + 1) * P],
                                        xw[:, gr * GW:(gr + 1) * GW], start=True, stop=True)
                    if i + 1 < TT:
                        ins.then_inc(ss_h, 1)
            for u in range(n_in, n_front):
                g = unit(u, g)
            pe.sem_inc(dn, 2)
            def turn_normed(tt):
                pe.wait_ge(h2_ok, tt + 1)
                if tt >= 2:
                    pe.wait_ge(h2_ev, tt - 1)
                for half in range(2):
                    for k in range(4):
                        ins = te.transpose(bank[2 + 2 * (tt % 2) + half][:, k * P:(k + 1) * P],
                                           X[:, tt, (4 * half + k) * P:(4 * half + k + 1) * P], ident[:, :])
                    ins.then_inc(h2_tr, 1)

            def route(tt):
                pe.wait_ge(h2_ev, tt + 1)
                if tt >= 2:
                    pe.wait_ge(h2_evb, tt - 1)
                ht = h2t[:, tt % 2, :].rearrange("p (k t) -> p k t", k=KD)
                for k in range(KD):
                    ins = te.matmul(bank[7][0:G + NE, tt * P:(tt + 1) * P], rt[:, k, :], ht[:, k, :],
                                    start=(k == 0), stop=(k == KD - 1))
                ins.then_inc(lg_t, 1)

            turn_normed(0)
            turn_normed(1)
            pe.wait_ge(rt_in, 32)
            route(0)
            turn_normed(2)
            route(1)
            turn_normed(3)
            route(2)
            route(3)
            pe.wait_ge(lg_c, 1)
            for tt in range(TT):
                ins = te.transpose(bank[6][:, tt * (G + NE):(tt + 1) * (G + NE)], lgf[:, tt * P:(tt + 1) * P],
                                   ident[0:G + NE, 0:G + NE])
            ins.then_inc(lg_mm, 1)
            keep_warm(20)
            pe.wait_ge(m_ok, 1)
            for tt in range(TT + 1):
                dst = bank[6][:, tt * NE:(tt + 1) * NE]
                for t2 in range(tt):
                    ins = te.matmul(dst, onesb, mb[:, t2, :], start=(t2 == 0), stop=(tt == TT and t2 == TT - 1))
                if tt < TT:
                    te.matmul(dst, before, mb[:, tt, :], start=(tt == 0), stop=True)
            ins.then_inc(pos_mm, 1)
            keep_warm(10)

            def find_tokens(step):
                pe.wait_ge(q_ok, step + 1)
                for tt in range(TT):
                    ins = te.matmul(bank[7][:, 0:2], onehot[:, tt, :], vale[:, tt, :], start=(tt == 0),
                                    stop=(tt == TT - 1))
                ins.then_inc(ix_mm, 1)

            def turn_tokens(step, b, uses):
                pe.wait_ge(gat_in[b], uses * 16)
                pe.wait_ge(gl_ok, step * 2 + 2)
                for half in range(2):
                    for k in range(4):
                        ins = te.transpose(bank[2 + half][:, k * P:(k + 1) * P],
                                           hg[:, b, (4 * half + k) * P:(4 * half + k + 1) * P], ident[:, :])
                    ins.then_inc(g_tr, 1)

            def gate_up(b, slot, ks, first, last):
                kh = KD // 2
                uh = wh[:, slot, :].rearrange("p (k n) -> p k n", k=kh)
                ul = wl[:, slot, :].rearrange("p (k n) -> p k n", k=kh)
                for k in ks:
                    kt = slot * kh + k
                    ah, al_ = gth[b][:, kt * P:(kt + 1) * P], gtl[b][:, kt * P:(kt + 1) * P]
                    te.matmul(bank[b][:, :], ah, uh[:, k, :], start=(first and k == 0), stop=False)
                    te.matmul(bank[b][:, :], ah, ul[:, k, :], start=False, stop=False)
                    ins = te.matmul(bank[b][:, :], al_, uh[:, k, :], start=False, stop=(last and k == kh - 1))
                return ins

            def gate_up_a1(step, b):
                pe.wait_ge(gl_ok, step * 2 + 4)
                pe.wait_ge(hid_ok, step)
                pe.wait_ge(wla_ok, step * 2 + 1)
                gate_up(b, 0, (0, 1), True, False)

            def gate_up_a2(step, b):
                pe.wait_ge(wla_ok, step * 2 + 2)
                gate_up(b, 0, (2, 3), False, False).then_inc(gu_a, 1)

            def pe_expert(e, step, b, uses, ahead1, ahead2):
                o = 1 - b
                if ahead1:
                    turn_tokens(step + 1, o, uses + b)
                if ahead2:
                    pe.wait_ge(ix_ok, step + 2)
                    find_tokens(step + 2)
                pe.wait_ge(wlb_ok, step * 2 + 2)
                gate_up(b, 1, range(4), False, True).then_inc(gu_b, 1)
                if ahead1:
                    gate_up_a1(step + 1, o)
                pe.wait_ge(hid_ok, step + 2)
                pe.wait_ge(hl_ok, step + 1)
                for k in range(2):
                    ins = te.transpose(bank[4][:, k * P:(k + 1) * P], hid[:, k * P:(k + 1) * P], ident[:, :])
                ins.then_inc(hid_tr, 1)
                if ahead1:
                    gate_up_a2(step + 1, o)
                pe.wait_ge(hl_ok, step + 2)
                pe.wait_ge(wlc_ok, step * 2 + 2)
                c3h = wch.rearrange("p (k n) -> p k n", k=2)
                c3l = wcl.rearrange("p (k n) -> p k n", k=2)
                for h in range(2):
                    pe.wait_ge(y0_ok if h == 0 else y1_ok, step + 1)
                    terms = []
                    for k in range(2):
                        c, n = slice(k * P, (k + 1) * P), slice(h * 512, (h + 1) * 512)
                        terms += [(hidh[:, c], c3h[:, k, n]), (hidh[:, c], c3l[:, k, n]), (hidl[:, c], c3h[:, k, n])]
                    products(bank[5 + h][:, :], terms).then_inc(dn, 1)

            def pe_round(r, base):
                used = r * PAIRS
                find_tokens(base)
                pe.wait_ge(ix_ok, base + 1)
                find_tokens(base + 1)
                keep_warm(14)
                turn_tokens(base, 0, used + 1)
                keep_warm(4)
                pe.wait_ge(gl_ok, base * 2 + 4)
                pe.wait_ge(wla_ok, base * 2 + 1)
                gate_up(0, 0, (0, 1), True, False)
                gate_up_a2(base, 0)
                with pe.Fori(0, PAIRS - 1) as pp:
                    for b in range(2):
                        pe_expert(pp * 2 + b, base + pp * 2 + b, b, used + pp + 1, True, True)
                pe_expert(NE - 2, base + NE - 2, 0, used + PAIRS, True, False)
                pe_expert(NE - 1, base + NE - 1, 1, used + PAIRS, False, False)

            expert_rounds(pe, pe_round)


_INS = ["x", "norm_mix_w", "w_in", "conv_w", "conv_b", "dt_bias", "a_log", "d_skip", "ssd_norm_w", "hgrn_lb_logits",
        "hgrn_norm_w", "w_out", "norm_ffn_w", "router_group", "router_expert", "w_gate", "w_up", "w_down",
        "final_norm_w"]


def kernel(**inputs):
    import numpy as np
    import concourse.bacc as bacc
    from concourse.bass_utils import run_bass_kernel_spmd

    nc = bacc.Bacc("TRN2", target_bir_lowering=False, num_devices=1, dynamic_dma_scratch_size=8192)
    arrays, args = {}, []
    for name in _INS:
        a = np.ascontiguousarray(inputs[name])
        arrays[f"in_{name}_dram"] = a
        args.append(nc.dram_tensor(f"in_{name}_dram", a.shape, mybir.dt.from_np(a.dtype), kind="ExternalInput").ap())
    shape = np.shape(inputs["x"])
    args.append(nc.dram_tensor("out_0_dram", shape, F32, kind="ExternalOutput").ap())
    trunk(nc, *args)
    r = run_bass_kernel_spmd(nc, [arrays], core_ids=[0])
    return r.results[0]["out_0_dram"]
```
